# Optimizing a Trainium2 kernel written in Bass

```python
import jax, jax.numpy as jnp
from jax import lax
import numpy as np

D_MODEL = 2048
BATCH = 1
SEQ = 256
DEPTH = 1

CHUNK = 64
Q_BLOCK = 128
N_MIXERS = 3
D_FF = 5632
FFN_RESIDUAL_WEIGHT = 0.5
RMS_EPS = 1e-6

A_HEADS = 8
A_QK_DIM = D_MODEL // (2 * A_HEADS)
A_V_DIM = D_MODEL // A_HEADS
A_IN = 2 * A_HEADS * A_QK_DIM + 2 * A_HEADS * A_V_DIM + 2 * A_HEADS
B_HEADS = 16
B_HEAD_DIM = D_MODEL // B_HEADS
B_IN = 3 * B_HEADS * B_HEAD_DIM + B_HEADS
C_HEADS = 4
C_K_DIM = D_MODEL // (2 * C_HEADS)
C_V_DIM = D_MODEL // C_HEADS
C_GATE_RANK = 16
C_GATE_TEMP = 16.0
C_IN = 2 * C_HEADS * C_K_DIM + 2 * C_HEADS * C_V_DIM + C_GATE_RANK

N_LAYERS_A = len(range(0, DEPTH, N_MIXERS))
N_LAYERS_B = len(range(1, DEPTH, N_MIXERS))
N_LAYERS_C = len(range(2, DEPTH, N_MIXERS))

kernel_name = "hybrid_mlstm_fox_gla_macaron_trunk"

def rmsnorm(x, g):
    xf = x.astype(jnp.float32)
    y = xf * lax.rsqrt(jnp.mean(xf * xf, axis=-1, keepdims=True) + RMS_EPS)
    return (y * g.astype(jnp.float32)).astype(x.dtype)

def head_rmsnorm(h, g):
    y = h * lax.rsqrt(jnp.mean(h * h, axis=-1, keepdims=True) + RMS_EPS)
    return y.reshape(h.shape[0], h.shape[1], -1) * g.astype(jnp.float32)

def swiglu_ffn(x, g, w_in, w_out):
    a, b = jnp.split(rmsnorm(x, g) @ w_in, 2, axis=-1)
    return (jax.nn.silu(a) * b) @ w_out

def to_chunks(t):
    b, s, h = t.shape[:3]
    t = t.reshape(b, s // CHUNK, CHUNK, h, *t.shape[3:])
    return jnp.moveaxis(t, (1, 3), (0, 2))

def from_chunks(t):
    t = jnp.moveaxis(t, (0, 2), (1, 3))
    return t.reshape(t.shape[0], t.shape[1] * t.shape[2], t.shape[3], t.shape[4])

def mlstm_chunk_step(carry, inp):
    c_prev, n_prev, m_prev = carry
    q, k, v, i_pre, log_f = inp
    tri = jnp.tril(jnp.ones((CHUNK, CHUNK), dtype=bool))
    b = jnp.cumsum(log_f, axis=-1)
    d_log = jnp.where(tri, b[..., :, None] - b[..., None, :] + i_pre[..., None, :], -jnp.inf)
    inter_log = b + m_prev[..., None]
    m_t = jnp.maximum(inter_log, jnp.max(d_log, axis=-1))
    d_w = jnp.exp(d_log - m_t[..., None])
    inter_w = jnp.exp(inter_log - m_t)
    s = jnp.einsum('bhtd,bhsd->bhts', q, k) * d_w
    num = jnp.einsum('bhts,bhse->bhte', s, v) + inter_w[..., None] * jnp.einsum('bhtd,bhde->bhte', q, c_prev)
    den = jnp.sum(s, axis=-1) + inter_w * jnp.einsum('bhtd,bhd->bht', q, n_prev)
    h = num / jnp.maximum(jnp.abs(den), jnp.exp(-m_t))[..., None]
    b_last = b[..., -1]
    g = b_last[..., None] - b + i_pre
    m_new = jnp.maximum(b_last + m_prev, jnp.max(g, axis=-1))
    w_c = jnp.exp(b_last + m_prev - m_new)
    w_s = jnp.exp(g - m_new[..., None])
    c_new = w_c[..., None, None] * c_prev + jnp.einsum('bhs,bhsd,bhse->bhde', w_s, k, v)
    n_new = w_c[..., None] * n_prev + jnp.einsum('bhs,bhsd->bhd', w_s, k)
    return (c_new, n_new, m_new), h

def mlstm_mixer(u, w_in, b_if, head_norm_g, w_out):
    bsz, s, _ = u.shape
    nq, nv = A_HEADS * A_QK_DIM, A_HEADS * A_V_DIM
    p = (u @ w_in).astype(jnp.float32)
    q, k, v, o, gi, gf = jnp.split(p, [nq, 2 * nq, 2 * nq + nv, 2 * nq + 2 * nv, 2 * nq + 2 * nv + A_HEADS], axis=-1)
    b_if = b_if.astype(jnp.float32)
    i_pre = gi + b_if[:A_HEADS]
    log_f = jax.nn.log_sigmoid(gf + b_if[A_HEADS:])
    q = q.reshape(bsz, s, A_HEADS, A_QK_DIM)
    k = k.reshape(bsz, s, A_HEADS, A_QK_DIM) * (A_QK_DIM ** -0.5)
    v = v.reshape(bsz, s, A_HEADS, A_V_DIM)
    init = (jnp.zeros((bsz, A_HEADS, A_QK_DIM, A_V_DIM), jnp.float32),
            jnp.zeros((bsz, A_HEADS, A_QK_DIM), jnp.float32),
            jnp.zeros((bsz, A_HEADS), jnp.float32))
    _, h = lax.scan(mlstm_chunk_step, init,
                    (to_chunks(q), to_chunks(k), to_chunks(v), to_chunks(i_pre), to_chunks(log_f)))
    h = head_rmsnorm(from_chunks(h), head_norm_g) * jax.nn.sigmoid(o)
    return h.astype(u.dtype) @ w_out

def fox_mixer(u, w_in, b_f, w_out):
    bsz, s, _ = u.shape
    nd = B_HEADS * B_HEAD_DIM
    q, k, v, gf = jnp.split(u @ w_in, [nd, 2 * nd, 3 * nd], axis=-1)
    q = q.reshape(bsz, s, B_HEADS, B_HEAD_DIM).transpose(0, 2, 1, 3)
    k = k.reshape(bsz, s, B_HEADS, B_HEAD_DIM).transpose(0, 2, 1, 3)
    v = v.reshape(bsz, s, B_HEADS, B_HEAD_DIM).transpose(0, 2, 1, 3)
    log_f = jax.nn.log_sigmoid(gf.astype(jnp.float32) + b_f.astype(jnp.float32))
    cum_f = jnp.cumsum(log_f, axis=1).transpose(0, 2, 1)
    scale = B_HEAD_DIM ** -0.5
    outs = []
    for blk in range(s // Q_BLOCK):
        lo, hi = blk * Q_BLOCK, (blk + 1) * Q_BLOCK
        logits = jnp.einsum('bhtd,bhsd->bhts', q[:, :, lo:hi], k[:, :, :hi],
                            preferred_element_type=jnp.float32) * scale
        logits = logits + cum_f[:, :, lo:hi, None] - cum_f[:, :, None, :hi]
        mask = (lo + jnp.arange(Q_BLOCK))[:, None] >= jnp.arange(hi)[None, :]
        probs = jax.nn.softmax(jnp.where(mask, logits, -jnp.inf), axis=-1)
        outs.append(jnp.einsum('bhts,bhsd->bhtd', probs.astype(v.dtype), v[:, :, :hi]))
    o = jnp.concatenate(outs, axis=2).transpose(0, 2, 1, 3).reshape(bsz, s, nd)
    return o @ w_out

def gla_chunk_step(state, inp):
    q, k, v, la = inp
    tri = jnp.tril(jnp.ones((CHUNK, CHUNK), dtype=bool))
    b = jnp.cumsum(la, axis=2)
    diff = b[:, :, :, None, :] - b[:, :, None, :, :]
    decay = jnp.exp(jnp.where(tri[:, :, None], diff, -jnp.inf))
    a = jnp.einsum('bhtd,bhsd,bhtsd->bhts', q, k, decay)
    o = jnp.einsum('bhts,bhse->bhte', a, v) + jnp.einsum('bhtd,bhde->bhte', q * jnp.exp(b), state)
    b_last = b[:, :, -1]
    state = jnp.exp(b_last)[..., None] * state + jnp.einsum(
        'bhsd,bhse->bhde', k * jnp.exp(b_last[:, :, None] - b), v)
    return state, o

def gla_mixer(u, w_in, w_alpha, b_alpha, head_norm_g, w_out):
    bsz, s, _ = u.shape
    nk, nv = C_HEADS * C_K_DIM, C_HEADS * C_V_DIM
    p = (u @ w_in).astype(jnp.float32)
    q, k, v, r, a_low = jnp.split(p, [nk, 2 * nk, 2 * nk + nv, 2 * nk + 2 * nv], axis=-1)
    log_alpha = jax.nn.log_sigmoid(a_low @ w_alpha.astype(jnp.float32) + b_alpha.astype(jnp.float32)) / C_GATE_TEMP
    q = q.reshape(bsz, s, C_HEADS, C_K_DIM) * (C_K_DIM ** -0.5)
    k = k.reshape(bsz, s, C_HEADS, C_K_DIM)
    v = v.reshape(bsz, s, C_HEADS, C_V_DIM)
    log_alpha = log_alpha.reshape(bsz, s, C_HEADS, C_K_DIM)
    init = jnp.zeros((bsz, C_HEADS, C_K_DIM, C_V_DIM), jnp.float32)
    _, o = lax.scan(gla_chunk_step, init,
                    (to_chunks(q), to_chunks(k), to_chunks(v), to_chunks(log_alpha)))
    h = head_rmsnorm(from_chunks(o), head_norm_g) * jax.nn.silu(r)
    return h.astype(u.dtype) @ w_out

def setup_inputs(seed: int = 0) -> dict:
    key = jax.random.key(seed)
    ks = jax.random.split(key, 24)
    f32 = jnp.float32
    nrm = lambda k, shape, fan_in: jax.random.normal(k, shape, f32) * (fan_in ** -0.5)
    gain = lambda k, shape: 1.0 + 0.02 * jax.random.normal(k, shape, f32)
    x = jax.random.normal(ks[0], (BATCH, SEQ, D_MODEL), f32)
    ffn_norm = gain(ks[1], (DEPTH, 2, D_MODEL))
    ffn_w_in = nrm(ks[2], (DEPTH, 2, D_MODEL, 2 * D_FF), D_MODEL)
    ffn_w_out = nrm(ks[3], (DEPTH, 2, D_FF, D_MODEL), D_FF)
    mix_norm = gain(ks[4], (DEPTH, D_MODEL))
    a_w_in = nrm(ks[5], (N_LAYERS_A, D_MODEL, A_IN), D_MODEL)
    a_b_if = jnp.concatenate([
        -2.0 + 0.1 * jax.random.normal(ks[6], (N_LAYERS_A, A_HEADS), f32),
        3.0 + 0.1 * jax.random.normal(ks[7], (N_LAYERS_A, A_HEADS), f32)], axis=-1)
    a_head_norm = gain(ks[8], (N_LAYERS_A, A_HEADS * A_V_DIM))
    a_w_out = nrm(ks[9], (N_LAYERS_A, A_HEADS * A_V_DIM, D_MODEL), A_HEADS * A_V_DIM)
    b_w_in = nrm(ks[10], (N_LAYERS_B, D_MODEL, B_IN), D_MODEL)
    b_b_f = 2.0 + 0.1 * jax.random.normal(ks[11], (N_LAYERS_B, B_HEADS), f32)
    b_w_out = nrm(ks[12], (N_LAYERS_B, B_HEADS * B_HEAD_DIM, D_MODEL), B_HEADS * B_HEAD_DIM)
    c_w_in = nrm(ks[13], (N_LAYERS_C, D_MODEL, C_IN), D_MODEL)
    c_w_alpha = nrm(ks[14], (N_LAYERS_C, C_GATE_RANK, C_HEADS * C_K_DIM), C_GATE_RANK)
    c_b_alpha = 0.1 * jax.random.normal(ks[15], (N_LAYERS_C, C_HEADS * C_K_DIM), f32)
    c_head_norm = gain(ks[16], (N_LAYERS_C, C_HEADS * C_V_DIM))
    c_w_out = nrm(ks[17], (N_LAYERS_C, C_HEADS * C_V_DIM, D_MODEL), C_HEADS * C_V_DIM)
    final_norm = gain(ks[18], (D_MODEL,))
    return {"x": x, "ffn_norm": ffn_norm, "ffn_w_in": ffn_w_in, "ffn_w_out": ffn_w_out,
            "mix_norm": mix_norm, "a_w_in": a_w_in, "a_b_if": a_b_if, "a_head_norm": a_head_norm,
            "a_w_out": a_w_out, "b_w_in": b_w_in, "b_b_f": b_b_f, "b_w_out": b_w_out,
            "c_w_in": c_w_in, "c_w_alpha": c_w_alpha, "c_b_alpha": c_b_alpha,
            "c_head_norm": c_head_norm, "c_w_out": c_w_out, "final_norm": final_norm}

def reference(x, ffn_norm, ffn_w_in, ffn_w_out, mix_norm, a_w_in, a_b_if, a_head_norm, a_w_out,
              b_w_in, b_b_f, b_w_out, c_w_in, c_w_alpha, c_b_alpha, c_head_norm, c_w_out, final_norm):
    h = x
    for i in range(DEPTH):
        h = h + FFN_RESIDUAL_WEIGHT * swiglu_ffn(h, ffn_norm[i, 0], ffn_w_in[i, 0], ffn_w_out[i, 0])
        u = rmsnorm(h, mix_norm[i])
        kind, j = i % N_MIXERS, i // N_MIXERS
        if kind == 0:
            y = mlstm_mixer(u, a_w_in[j], a_b_if[j], a_head_norm[j], a_w_out[j])
        elif kind == 1:
            y = fox_mixer(u, b_w_in[j], b_b_f[j], b_w_out[j])
        else:
            y = gla_mixer(u, c_w_in[j], c_w_alpha[j], c_b_alpha[j], c_head_norm[j], c_w_out[j])
        h = h + y
        h = h + FFN_RESIDUAL_WEIGHT * swiglu_ffn(h, ffn_norm[i, 1], ffn_w_in[i, 1], ffn_w_out[i, 1])
    return rmsnorm(h, final_norm)


_drawn_inputs = setup_inputs


def setup_inputs(seed=0):
    import zlib

    import numpy as np

    out = dict(_drawn_inputs(seed))
    spreads = {}
    factors = {'ffn_norm': 4.062, 'a_head_norm': 5.997, 'final_norm': 2.839}
    for name, (base, spread) in spreads.items():
        noise = np.random.default_rng([zlib.crc32(name.encode()), seed]).standard_normal(out[name].shape)
        drawn = base * np.exp(spread * noise) if base else spread * noise
        out[name] = __import__('jax').numpy.asarray(drawn.astype(out[name].dtype))
    for name, factor in factors.items():
        out[name] = (out[name] * factor).astype(out[name].dtype)
    return out
```

```python
from contextlib import ExitStack

import concourse.bass as bass
from concourse import mybir

F32 = mybir.dt.float32
F32R = mybir.dt.float32r
ALU = mybir.AluOpType
ACT = mybir.ActivationFunctionType
AXX = mybir.AxisListType.X

P = 128
COLS = 512
GK = 2
RING = 4
EPS = 1e-6


def trunk_program(nc, x, ffn_norm, ffn_w_in, ffn_w_out, mix_norm, a_w_in, a_b_if, a_head_norm,
                  a_w_out, final_norm, out):
    _, SEQ, D = x.shape
    FF = ffn_w_out.shape[2]
    HEADS = a_b_if.shape[1] // 2
    QK = D // (2 * HEADS)
    VD = D // HEADS
    TT = SEQ // P
    KD, KF = D // P, FF // P
    ND, NF = D // COLS, FF // COLS
    GD, GF = KD // GK, KF // GK
    NQ, NV = HEADS * QK // COLS, HEADS * VD // COLS
    K_SCALE = QK ** -0.5
    assert TT == 2 and QK == P and VD == 2 * P and GD == 8 and GD % RING == 0 and 2 * GF % RING == 0

    C_FFN, C_FFN_OUT = (0, 2 * NF + 2 * ND + 2 * NQ + 2 * NV), None
    C_FFN_OUT = tuple(c + 2 * NF for c in C_FFN)
    C_MIX = C_FFN_OUT[0] + ND
    C_MIX_OUT = C_MIX + 2 * NQ + 2 * NV
    G_FFN = (0, 2 * NF * GD + ND * GF + (2 * NQ + 2 * NV + ND) * GD)
    G_FFN_OUT = tuple(g + 2 * NF * GD for g in G_FFN)
    G_MIX = G_FFN_OUT[0] + ND * GF
    G_MIX_OUT = G_MIX + (2 * NQ + 2 * NV) * GD
    assert C_FFN[1] == C_MIX_OUT + ND and G_FFN[1] == G_MIX_OUT + ND * GD
    R_X = 0
    R_HID1 = R_X + ND
    R_H1 = R_HID1 + NF
    R_QK = R_H1 + ND
    R_Y = R_QK + 2 * NQ
    R_H2 = R_Y + NV
    R_HID2 = R_H2 + ND
    R_H3 = R_HID2 + NF
    R_HID = (R_HID1, R_HID2)
    SILUS = (0, NF + NV)

    with ExitStack() as ctx:
        def sb(name, shape, dt=F32):
            return ctx.enter_context(nc.sbuf_tensor(name, shape, dt))

        def sem(name):
            return ctx.enter_context(nc.semaphore(name))

        h = sb("h", [P, TT, D])
        u_hi = sb("u_hi", [P, KD, SEQ], F32R)
        u_lo = sb("u_lo", [P, KD, SEQ], F32R)
        raw = sb("raw", [P, RING, GK, COLS])
        w_hi = sb("w_hi", [P, RING, GK, COLS], F32R)
        w_lo = sb("w_lo", [P, RING, GK, COLS], F32R)
        tile = sb("tile", [P, TT, COLS])
        final_gain = sb("final_gain", [P, D])
        ident = sb("ident", [P, P])
        gain_rows = sb("gain_rows", [4 * KD, P])
        gains = sb("gains", [P, 4 * KD])
        squares = sb("squares", [P, 4, TT, ND])
        mean_sq = sb("mean_sq", [P, 4, TT])
        root = sb("root", [P, 4, TT])
        root_sq = sb("root_sq", [P, 4, TT])
        rstd = sb("rstd", [P, 4, TT])
        with ExitStack() as mixer_place:
            def mx(name, shape, dt=F32):
                return mixer_place.enter_context(nc.sbuf_tensor(name, shape, dt))

            y_hi = mx("y_hi", [P, KD, SEQ], F32R)
            y_lo = mx("y_lo", [P, KD, SEQ], F32R)
            q_t = mx("q_t", [P, HEADS, SEQ])
            k_t = mx("k_t", [P, HEADS, SEQ])
            v = mx("v", [P, TT, HEADS * VD])
            heads_out = mx("heads_out", [P, TT, COLS])
            f_pre = mx("f_pre", [HEADS, SEQ])
            f_abs = mx("f_abs", [HEADS, SEQ])
            A = mx("A", [HEADS, SEQ])
            M = mx("M", [HEADS, SEQ])
            B = mx("B", [HEADS, SEQ])
            decay = mx("decay", [P, 3 * P])
            weighted = mx("weighted", [P, 3 * P])
            scratch_v = mx("scratch_v", [P, VD])
        with ExitStack() as hidden_place:
            def hd(name, shape, dt=F32):
                return hidden_place.enter_context(nc.sbuf_tensor(name, shape, dt))

            g_hi = hd("g_hi", [P, KF, SEQ], F32R)
            g_lo = hd("g_lo", [P, KF, SEQ], F32R)
        ctx.enter_context(nc.sbuf_tensor("hidden_fence", [P, 2 * KF, SEQ], F32))
        gw = sb("gw", [P, KD, 2 * HEADS])
        gw_hi = sb("gw_hi", [P, KD, 2 * HEADS], F32R)
        gw_lo = sb("gw_lo", [P, KD, 2 * HEADS], F32R)
        gate_bias = sb("gate_bias", [HEADS, 2])
        gates = sb("gates", [P, TT, 2 * HEADS])
        select = sb("select", [HEADS, HEADS, P])
        ones = sb("ones", [P, 1])
        A_t = sb("A_t", [P, TT, HEADS])
        floor_t = sb("floor_t", [P, TT, HEADS])
        den = sb("den", [P, TT])
        den_inv = sb("den_inv", [P, TT])
        head_sq = sb("head_sq", [P, TT])
        head_root = sb("head_root", [P, TT])
        head_root_sq = sb("head_root_sq", [P, TT])
        head_rstd = sb("head_rstd", [P, TT])
        scratch = sb("scratch", [P, COLS])

        acc = ctx.enter_context(nc.psum_tensor("acc", [P, 2 * TT, COLS], F32))
        aux = [ctx.enter_context(nc.psum_tensor(f"aux{i}", [P, COLS], F32)) for i in range(4)]
        bcast_ps, scores_ps, num_ps, turn_ps = aux
        den_ps = bcast_ps[:, SEQ:SEQ + TT]

        x_landed = [sem(f"x_landed{n}") for n in range(ND)]
        gains_landed = sem("gains_landed")
        gw_landed = sem("gw_landed")
        bias_landed = sem("bias_landed")
        final_gain_landed = sem("final_gain_landed")
        raw_landed = [sem(f"raw_landed{i}") for i in range(RING)]
        high_ready = sem("high_ready")
        low_ready = sem("low_ready")
        granules_used = sem("granules_used")
        tile_ready = sem("tile_ready")
        turned = sem("turned")
        turned_high = sem("turned_high")
        turned_low = sem("turned_low")
        squared = sem("squared")
        kept = sem("kept")
        silu_ready = sem("silu_ready")
        mean_ready = sem("mean_ready")
        root_log = sem("root_log")
        root_ready = sem("root_ready")
        rstd_ready = sem("rstd_ready")
        consts_ready = sem("consts_ready")
        gain_turned = sem("gain_turned")
        gains_ready = sem("gains_ready")
        gw_high_ready = sem("gw_high_ready")
        gw_ready = sem("gw_ready")
        v_ready = sem("v_ready")
        gates_summed = sem("gates_summed")
        gates_ready = sem("gates_ready")
        gates_turned = sem("gates_turned")
        f_ready = sem("f_ready")
        exp_f = sem("exp_f")
        log_ready = sem("log_ready")
        stab_ready = sem("stab_ready")
        stab_turned = sem("stab_turned")
        A_t_ready = sem("A_t_ready")
        floor_ready = sem("floor_ready")
        scores_ready = sem("scores_ready")
        decay_ready = sem("decay_ready")
        decay_masked = sem("decay_masked")
        weighted_ready = sem("weighted_ready")
        num_ready = sem("num_ready")
        head_divided = sem("head_divided")
        head_root_ready = sem("head_root_ready")
        head_ready = sem("head_ready")
        vector_step = sem("vector_step")
        act_out = sem("act_out")
        vec_out = sem("vec_out")
        out_stored = sem("out_stored")

        w_in = [ffn_w_in[0, i].rearrange("(k p) n -> p k n", p=P) for i in range(2)]
        w_out = [ffn_w_out[0, i].rearrange("(k p) n -> p k n", p=P) for i in range(2)]
        mix_in = a_w_in[0].rearrange("(k p) n -> p k n", p=P)
        mix_out = a_w_out[0].rearrange("(k p) n -> p k n", p=P)
        x_tokens = x[0].rearrange("(t p) n -> p t n", p=P)
        out_tokens = out[0].rearrange("(t p) n -> p t n", p=P)
        GAIN_FFN = (0, 2 * KD)
        GAIN_MIX, GAIN_HEAD = KD, 3 * KD

        block = ctx.enter_context(nc.Block())

        @block.sync
        def _(sp):
            def load(w, g, more, k0, col):
                if g >= RING:
                    sp.wait_ge(low_ready, g - RING + 1 + more)
                sp.dma_start(raw[:, g % RING], w[:, k0:k0 + GK, bass.ds(col, COLS)])\
                    .then_inc(raw_landed[g % RING], 16)

            def load_pair(w, g, more, col0, col1, granules):
                for i in range(granules):
                    load(w, g + i, more, GK * i, col0)
                for i in range(granules):
                    load(w, g + granules + i, more, GK * i, col1)

            for n in range(ND):
                sp.dma_start(h[:, :, n * COLS:(n + 1) * COLS], x_tokens[:, :, n * COLS:(n + 1) * COLS])\
                    .then_inc(x_landed[n], 16)
                load(w_in[0], n, 0, GK * n, 0)
            for i in range(ND, GD):
                load(w_in[0], i, 0, GK * i, 0)
            for i in range(GD):
                load(w_in[0], GD + i, 0, GK * i, FF)
            with sp.Fori(0, NF - 1) as j:
                load_pair(w_in[0], G_FFN[0] + 2 * GD, 2 * GD * j, j * COLS + COLS,
                          j * COLS + (COLS + FF), GD)
            with sp.Fori(0, ND // 2) as m:
                load_pair(w_out[0], G_FFN_OUT[0], 2 * GF * m, 2 * COLS * m, 2 * COLS * m + COLS, GF)
            with sp.Fori(0, NQ + NV) as m:
                load_pair(mix_in, G_MIX, 2 * GD * m, 2 * COLS * m, 2 * COLS * m + COLS, GD)
            with sp.Fori(0, ND // 2) as m:
                load_pair(mix_out, G_MIX_OUT, 2 * GD * m, 2 * COLS * m, 2 * COLS * m + COLS, GD)
            with sp.Fori(0, NF) as j:
                load_pair(w_in[1], G_FFN[1], 2 * GD * j, j * COLS, j * COLS + FF, GD)
            with sp.Fori(0, ND // 2) as m:
                load_pair(w_out[1], G_FFN_OUT[1], 2 * GF * m, 2 * COLS * m, 2 * COLS * m + COLS, GF)

            last = (ND - 1) * COLS
            sp.wait_ge(vec_out, 1)
            sp.dma_start(out_tokens[:, :, last:], tile[:, :, :]).then_inc(out_stored, 16)
            sp.wait_ge(act_out, 1)
            sp.dma_start(out_tokens[:, 0, :last], h[:, 0, :last]).then_inc(out_stored, 16)
            sp.wait_ge(vec_out, 2)
            sp.dma_start(out_tokens[:, 1, :last], h[:, 1, :last]).then_inc(out_stored, 16)
            sp.wait_ge(out_stored, 48)

        @block.gpsimd
        def _(pool):
            nc.gpsimd.memset(ident[:, :], 0.0).then_inc(consts_ready, 1)
            nc.gpsimd.memset(select[:, :, :], 1.0).then_inc(consts_ready, 1)
            nc.gpsimd.memset(ones[:, :], 1.0).then_inc(consts_ready, 1)
            pool.wait_ge(consts_ready, 3)
            nc.gpsimd.affine_select(out=ident[:, :], in_=ident[:, :], compare_op=ALU.not_equal, fill=1.0,
                                    base=0, pattern=[[-1, P]], channel_multiplier=1)\
                .then_inc(consts_ready, 1)
            nc.gpsimd.affine_select(out=select[:, :, :], in_=select[:, :, :], compare_op=ALU.is_equal,
                                    fill=0.0, base=0, pattern=[[-1, HEADS], [0, P]],
                                    channel_multiplier=1).then_inc(consts_ready, 1)
            pool.dma_start(gw[:, :, :], mix_in[:, :, 2 * (NQ + NV) * COLS:]).then_inc(gw_landed, 16)
            pool.dma_start(gate_bias[:, :], a_b_if[0].rearrange("(a h) -> h a", a=2),
                           allow_slow_non_contiguous=True)\
                .then_inc(bias_landed, 16)
            pool.dma_start(final_gain[:, :], final_norm.partition_broadcast(P))\
                .then_inc(final_gain_landed, 16)

            def keep(turn_, n, phase):
                pool.wait_ge(tile_ready, turn_ - R_HID1 + 1)
                nc.gpsimd.tensor_copy(h[:, :, n * COLS:(n + 1) * COLS], tile[:, :, :])\
                    .then_inc(kept, 1)

            for n in range(ND):
                keep(R_H1 + n, n, 0)

            for hd_ in range(HEADS):
                pool.wait_ge(decay_ready, hd_ + 1)
                for at in (0, 2 * P):
                    last = nc.gpsimd.affine_select(out=decay[:, at:at + P], in_=decay[:, at:at + P],
                                                   compare_op=ALU.is_ge, fill=0.0, base=0,
                                                   pattern=[[1, P]], channel_multiplier=-1)
                last.then_inc(decay_masked, 1)

            for n in range(ND):
                keep(R_H2 + n, n, 1)
            pool.wait_ge(final_gain_landed, 16)
            for n in range(ND - 1):
                cols = slice(n * COLS, (n + 1) * COLS)
                pool.wait_ge(tile_ready, R_H3 + n - R_HID1 + 1)
                for t in range(TT):
                    last = nc.gpsimd.tensor_tensor(h[:, t, cols], tile[:, t, :], final_gain[:, cols],
                                                   ALU.mult)
                last.then_inc(kept, 1)

        @block.tensor
        def _(pe):

            def run(c, g, more, first, last, granules, s_hi, s_lo, need=None):
                for i in range(first, last):
                    if need is not None:
                        pe.wait_ge(turned_low, 2 * need + i + 1)
                    pe.wait_ge(low_ready, g + i + 1 + more)
                    ring = (g + i) % RING
                    for kk in range(GK):
                        k = GK * i + kk
                        for t in range(TT):
                            tok = slice(t * P, (t + 1) * P)
                            for n, (s, w) in enumerate(((s_hi, w_hi), (s_hi, w_lo), (s_lo, w_hi))):
                                mm = nc.tensor.matmul(acc[:, TT * (c % 2) + t, :], s[:, k, tok],
                                                      w[:, ring, kk, :],
                                                      start=(k == 0 and n == 0),
                                                      stop=(k == GK * granules - 1 and n == 2))
                    mm.then_inc(granules_used, 1)

            def turn(r, more, half, src=None, ps=None):
                if half == 0 and src is None:
                    pe.wait_ge(tile_ready, r - R_HID1 + 1 + more)
                if ps is None:
                    pe.wait_ge(turned_low, 2 * r + half + more * 2)
                for kk in range(2):
                    for t in range(TT):
                        a = (2 * half + kk) * P
                        block_ = tile[:, t, a:a + P] if src is None else h[:, t, src + a:src + a + P]
                        mm = nc.tensor.transpose((turn_ps if ps is None else ps)[:, kk * SEQ + t * P:
                                                                                   kk * SEQ + (t + 1) * P],
                                                 block_, ident[:, :])
                mm.then_inc(turned, 1)

            def chunk_turn(c, g, granules, s_hi, s_lo, r, gm=0, rm=0, wait_from=None):
                run(c, g, gm, 0, 2, granules, s_hi, s_lo)
                turn(r, rm, 0)
                run(c, g, gm, 2, 4, granules, s_hi, s_lo)
                turn(r, rm, 1)
                if wait_from is None:
                    run(c, g, gm, 4, granules, granules, s_hi, s_lo)
                else:
                    run(c, g, gm, 4, wait_from, granules, s_hi, s_lo)
                    pe.wait_ge(turned_low, 2 * r + 1 + 2 * rm)
                    run(c, g, gm, wait_from, wait_from + 1, granules, s_hi, s_lo)
                    pe.wait_ge(turned_low, 2 * r + 2 + 2 * rm)
                    run(c, g, gm, wait_from + 1, granules, granules, s_hi, s_lo)

            def ffn_out_turned():
                pe.wait_ge(silu_ready, NF)
                with pe.Fori(0, ND // 2) as m:
                    chunk_turn(C_FFN_OUT[0], G_FFN_OUT[0], GF, g_hi, g_lo, R_HID1 + NF - 1,
                               gm=2 * GF * m, rm=2 * m, wait_from=GF - 2)
                    chunk_turn(C_FFN_OUT[0] + 1, G_FFN_OUT[0] + GF, GF, g_hi, g_lo, R_HID1 + NF,
                               gm=2 * GF * m, rm=2 * m)

            def ffn_out_last():
                c, g = C_FFN_OUT[1], G_FFN_OUT[1]
                pe.wait_ge(silu_ready, 2 * NF + NV)
                chunk_turn(c, g, GF, g_hi, g_lo, R_HID2 + NF - 1, wait_from=GF - 2)
                for n in range(1, ND):
                    if n >= 2:
                        pe.wait_ge(tile_ready, R_H3 + n - 2 - R_HID1 + 1)
                    run(c + n, g + n * GF, 0, 0, GF, GF, g_hi, g_lo)

            def ffn_in_rest(i):
                c, g, r = C_FFN[i], G_FFN[i], R_HID[i]
                with pe.Fori(0, NF - 1) as j:
                    run(c + 1, g + GD, 2 * GD * j, 0, GD, GD, u_hi, u_lo)
                    pe.wait_ge(silu_ready, SILUS[i] + 1 + j)
                    chunk_turn(c + 2, g + 2 * GD, GD, u_hi, u_lo, r, gm=2 * GD * j, rm=j)
                run(c + 2 * NF - 1, g + (2 * NF - 1) * GD, 0, 0, GD, GD, u_hi, u_lo)

            pe.wait_ge(consts_ready, 4)
            pe.wait_ge(gains_landed, 64)
            nc.tensor.transpose(acc[:, 0, 0:4 * KD], gain_rows[:, :], ident[0:4 * KD, 0:4 * KD])\
                .then_inc(gain_turned, 1)
            for n in range(ND):
                pe.wait_ge(x_landed[n], 16)
                for half in range(2):
                    q = 2 * n + half
                    if q >= len(aux):
                        pe.wait_ge(turned_low, q - len(aux) + 1)
                    turn(n, 0, half, src=n * COLS, ps=aux[q % len(aux)])
            pe.wait_ge(gains_ready, 1)
            run(C_FFN[0], G_FFN[0], 0, 0, GD, GD, u_hi, u_lo, need=R_X)
            ffn_in_rest(0)
            ffn_out_turned()

            def mix(n):
                return C_MIX + n, G_MIX + n * GD

            c, g = mix(0)
            chunk_turn(c, g, GD, u_hi, u_lo, R_H1 + ND - 1, wait_from=GD - 2)
            c, g = mix(1)
            run(c, g, 0, 0, 2, GD, u_hi, u_lo)
            turn(R_QK, 0, 0)
            run(c, g, 0, 2, 4, GD, u_hi, u_lo)
            turn(R_QK, 0, 1)
            run(c, g, 0, 4, 6, GD, u_hi, u_lo)
            pe.wait_ge(gw_ready, 1)
            for t in range(TT):
                tok = slice(t * P, (t + 1) * P)
                for k in range(KD):
                    for n, (s, w) in enumerate(((u_hi, gw_hi), (u_hi, gw_lo), (u_lo, gw_hi))):
                        mm = nc.tensor.matmul(bcast_ps[:, t * 2 * HEADS:(t + 1) * 2 * HEADS],
                                              s[:, k, tok], w[:, k, :],
                                              start=(k == 0 and n == 0), stop=(k == KD - 1 and n == 2))
            mm.then_inc(gates_summed, 1)
            run(c, g, 0, 6, GD, GD, u_hi, u_lo)
            c, g = mix(2)
            chunk_turn(c, g, GD, u_hi, u_lo, R_QK + 1)
            pe.wait_ge(gates_ready, 1)
            for a in range(2):
                for t in range(TT):
                    mm = nc.tensor.transpose(scores_ps[0:HEADS, a * SEQ + t * P:a * SEQ + (t + 1) * P],
                                             gates[:, t, a * HEADS:(a + 1) * HEADS], ident[:, :])
            mm.then_inc(gates_turned, 1)
            c, g = mix(3)
            chunk_turn(c, g, GD, u_hi, u_lo, R_QK + 2)
            c, g = mix(4)
            chunk_turn(c, g, GD, u_hi, u_lo, R_QK + 3)
            pe.wait_ge(stab_ready, 1)
            for a, row in enumerate((A, B)):
                for t in range(TT):
                    mm = nc.tensor.transpose(bcast_ps[:, (t * 2 + a) * HEADS:(t * 2 + a + 1) * HEADS],
                                             row[:, t * P:(t + 1) * P], ident[0:HEADS, 0:HEADS])
            mm.then_inc(stab_turned, 1)
            for n in range(5, 8):
                c, g = mix(n)
                if n >= 6:
                    pe.wait_ge(v_ready, n - 5)
                run(c, g, 0, 0, GD, GD, u_hi, u_lo)

            def head_scores(hd_):
                if hd_ == 0:
                    pe.wait_ge(A_t_ready, 1)
                    pe.wait_ge(floor_ready, 1)
                else:
                    pe.wait_ge(head_divided, hd_)
                nc.tensor.matmul(bcast_ps[:, 0:SEQ], select[:, hd_, :], M[:, :], start=True, stop=True)
                nc.tensor.matmul(scores_ps[:, 0:SEQ], k_t[:, hd_, 0:P], q_t[:, hd_, :],
                                 start=True, stop=True)
                nc.tensor.matmul(scores_ps[:, SEQ:SEQ + P], k_t[:, hd_, P:SEQ], q_t[:, hd_, P:SEQ],
                                 start=True, stop=True).then_inc(scores_ready, 1)

            def head_sums(hd_):
                pe.wait_ge(weighted_ready, hd_ + 1)
                cols = slice(hd_ * VD, (hd_ + 1) * VD)
                for t, parts in ((0, ((0, 0),)), (1, ((P, 0), (2 * P, 1)))):
                    for n, (at, s) in enumerate(parts):
                        first, last = n == 0, n == len(parts) - 1
                        nc.tensor.matmul(num_ps[:, t * VD:(t + 1) * VD], weighted[:, at:at + P],
                                         v[:, s, cols], start=first, stop=last)
                        mm = nc.tensor.matmul(den_ps[:, t:t + 1], weighted[:, at:at + P], ones[:, :],
                                              start=first, stop=last)
                mm.then_inc(num_ready, 1)

            for p in range(NV):
                c, g = mix(8 + p)
                if p < 2:
                    pe.wait_ge(v_ready, NV - 1 + p)
                run(c, g, 0, 0, 1, GD, u_hi, u_lo)
                head_scores(2 * p)
                run(c, g, 0, 1, 2, GD, u_hi, u_lo)
                if p:
                    turn(R_Y + p - 1, 0, 0)
                run(c, g, 0, 2, 3, GD, u_hi, u_lo)
                if p == 0:
                    pe.wait_ge(v_ready, NV)
                head_sums(2 * p)
                run(c, g, 0, 3, 4, GD, u_hi, u_lo)
                if p:
                    turn(R_Y + p - 1, 0, 1)
                run(c, g, 0, 4, 5, GD, u_hi, u_lo)
                head_scores(2 * p + 1)
                run(c, g, 0, 5, 7, GD, u_hi, u_lo)
                head_sums(2 * p + 1)
                run(c, g, 0, 7, 8, GD, u_hi, u_lo)
            with pe.Fori(0, ND // 2) as m:
                chunk_turn(C_MIX_OUT, G_MIX_OUT, GD, y_hi, y_lo, R_Y + NV - 1,
                           gm=2 * GD * m, rm=2 * m, wait_from=GD - 2)
                chunk_turn(C_MIX_OUT + 1, G_MIX_OUT + GD, GD, y_hi, y_lo, R_Y + NV,
                           gm=2 * GD * m, rm=2 * m)

            chunk_turn(C_FFN[1], G_FFN[1], GD, u_hi, u_lo, R_H2 + ND - 1, wait_from=GD - 2)
            ffn_in_rest(1)
            ffn_out_last()

        @block.scalar
        def _(act):
            def split(g, first, last, more=0):
                for i in range(first, last):
                    n = g + i
                    act.wait_ge(raw_landed[n % RING], 16 * (n // RING + 1) + 16 // RING * more)
                    if n >= RING:
                        act.wait_ge(granules_used, n - RING + 1 + more)
                    nc.scalar.activation(w_hi[:, n % RING], raw[:, n % RING], ACT.Copy)\
                        .then_inc(high_ready, 1)

            def high(r, half, dst, gain=None, ps=None, more=0):
                act.wait_ge(turned, 2 * r + half + 1 + 2 * more)
                ps = turn_ps if ps is None else ps
                if gain is None:
                    last = nc.scalar.activation(dst, ps[:, :].rearrange("p (k t) -> p k t", k=2), ACT.Copy)
                else:
                    for kk in range(2):
                        last = nc.scalar.activation(dst[:, kk], ps[:, kk * SEQ:(kk + 1) * SEQ], ACT.Copy,
                                                    scale=gains[:, gain + kk:gain + kk + 1])
                last.then_inc(turned_high, 1)

            def high_h(r, n, half, gain, ps=None):
                k = 4 * n + 2 * half
                high(r, half, u_hi[:, k:k + 2], gain + k, ps)

            def square(norm, n, r):
                if r is None:
                    act.wait_ge(x_landed[n], 16)
                else:
                    act.wait_ge(tile_ready, r - R_HID1 + 1)
                for t in range(TT):
                    src = h[:, t, n * COLS:(n + 1) * COLS] if r is None else tile[:, t, :]
                    done = TT * (ND * norm + n) + t
                    if done:
                        act.wait_ge(squared, done)
                    nc.scalar.activation(scratch[:, :], src, ACT.Square,
                                         accum_out=squares[:, norm, t, n:n + 1]).then_inc(squared, 1)

            logs = [0]

            def inverse_root(y, x_):
                logs[0] += 1
                nc.scalar.activation(y, x_, ACT.Ln).then_inc(root_log, 1)
                act.wait_ge(root_log, logs[0])
                return nc.scalar.activation(y, y, ACT.Exp, scale=-0.5)

            def rms_root(norm):
                act.wait_ge(mean_ready, norm + 1)
                inverse_root(root[:, norm, :], mean_sq[:, norm, :]).then_inc(root_ready, 1)

            def silu(i, c, g_end, r, gm=0, rm=0):
                act.wait_ge(granules_used, g_end + gm)
                act.wait_ge(turned, 2 * r + 2 * rm)
                for t in range(TT):
                    last = nc.scalar.activation(tile[:, t, :], acc[:, TT * (c % 2) + t, :], ACT.Silu,
                                                scale=rstd[:, 2 * i, t:t + 1])
                last.then_inc(silu_ready, 1)

            def ffn_in(i):
                c, g, r = C_FFN[i], G_FFN[i], R_HID[i]
                act.wait_ge(rstd_ready, 2 * i + 1)
                if i:
                    act.wait_ge(kept, 2 * ND)
                with act.Fori(0, NF - 1) as j:
                    split(g + GD, 0, 3, 2 * GD * j)
                    silu(i, c, g + GD, r, gm=2 * GD * j, rm=j)
                    split(g + GD, 3, 8 + 5, 2 * GD * j)
                    high(r, 0, g_hi[:, bass.ds(4 * j, 2)], more=j)
                    split(g + 2 * GD, 5, 7, 2 * GD * j)
                    high(r, 1, g_hi[:, bass.ds(4 * j + 2, 2)], more=j)
                    split(g + 2 * GD, 7, 8, 2 * GD * j)
                g_b = g + (2 * NF - 1) * GD
                split(g_b, 0, 3)
                silu(i, c, g_b, r + NF - 1)
                split(g_b, 3, 8)

            def ffn_out(i):
                g, r = G_FFN_OUT[i], R_HID[i] + NF - 1
                split(g, 0, 5)
                high(r, 0, g_hi[:, KF - 4:KF - 2])
                split(g, 5, 7)
                high(r, 1, g_hi[:, KF - 2:KF])
                split(g, 7, GF)
                for n in range(1, ND):
                    g, r = g + GF, r + 1
                    split(g, 0, 3)
                    square(2 * i + 1, n - 1, r)
                    if i == 0:
                        split(g, 3, 5)
                        high_h(r, n - 1, 0, GAIN_MIX)
                        split(g, 5, 7)
                        high_h(r, n - 1, 1, GAIN_MIX)
                        split(g, 7, GF)
                    else:
                        split(g, 3, GF)

            def first_chunk(g, norm, r, gain):
                split(g, 0, 3)
                square(norm, ND - 1, r)
                split(g, 3, 5)
                high_h(r, ND - 1, 0, gain)
                split(g, 5, 7)
                high_h(r, ND - 1, 1, gain)
                rms_root(norm)
                split(g, 7, 8)

            for n, vector in enumerate((ffn_norm[0, 0], mix_norm[0], ffn_norm[0, 1], a_head_norm[0])):
                act.dma_start(gain_rows[n * KD:(n + 1) * KD, :], vector.rearrange("(k p) -> k p", p=P))\
                    .then_inc(gains_landed, 16)
            act.wait_ge(gain_turned, 1)
            nc.scalar.activation(gains[:, :], acc[:, 0, 0:4 * KD], ACT.Copy).then_inc(gains_ready, 1)
            act.wait_ge(gains_ready, 1)
            for n in range(ND):
                for half in range(2):
                    high_h(n, n, half, GAIN_FFN[0], aux[(2 * n + half) % len(aux)])
                split(0, n, n + 1)
            for n in range(ND):
                square(0, n, None)
            rms_root(0)
            split(0, 4, 8)
            act.wait_ge(gw_landed, 16)
            nc.scalar.activation(gw_hi[:, :, :], gw[:, :, :], ACT.Copy).then_inc(gw_high_ready, 1)
            ffn_in(0)
            ffn_out(0)

            def store_qk(n, half):
                act.wait_ge(turned, 2 * (R_QK + n) + half + 1)
                dst, head = (q_t, 4 * n) if n < NQ else (k_t, 4 * (n - NQ))
                nc.scalar.activation(dst[:, head + 2 * half], turn_ps[:, 0:SEQ], ACT.Copy,
                                     scale=1.0 if n < NQ else K_SCALE).then_inc(turned_high, 1)

            first_chunk(G_MIX, 1, R_H1 + ND - 1, GAIN_MIX)
            for n in range(1, 5):
                g = G_MIX + n * GD
                split(g, 0, 1)
                if n == 3:
                    act.wait_ge(f_ready, 2)
                    nc.scalar.activation(f_abs[:, :], f_abs[:, :], ACT.Exp, scale=-1.0).then_inc(exp_f, 1)
                    act.wait_ge(exp_f, 1)
                    nc.scalar.activation(f_abs[:, :], f_abs[:, :], ACT.Ln, bias=1.0).then_inc(log_ready, 1)
                split(g, 1, 5)
                store_qk(n - 1, 0)
                split(g, 5, 7)
                store_qk(n - 1, 1)
                split(g, 7, 8)

            act.wait_ge(rstd_ready, 2)

            def store_v(n):
                g_end = G_MIX + (5 + n) * GD
                act.wait_ge(granules_used, g_end)
                for t in range(TT):
                    last = nc.scalar.activation(v[:, t, n * COLS:(n + 1) * COLS],
                                                acc[:, TT * ((C_MIX + 4 + n) % 2) + t, :], ACT.Copy,
                                                scale=rstd[:, 1, t:t + 1])
                last.then_inc(v_ready, 1)

            for n in range(5, 8):
                g = G_MIX + n * GD
                split(g, 0, 1)
                if n == 5:
                    act.wait_ge(stab_turned, 1)
                    for t in range(TT):
                        at = (2 * t + 1) * HEADS
                        last = nc.scalar.activation(floor_t[:, t, :], bcast_ps[:, at:at + HEADS], ACT.Exp,
                                                    scale=-1.0)
                    last.then_inc(floor_ready, 1)
                split(g, 1, 3)
                store_v(n - 5)
                split(g, 3, 8)

            def head_decay(hd_):
                act.wait_ge(scores_ready, hd_ + 1)
                if hd_:
                    act.wait_ge(weighted_ready, hd_)
                else:
                    act.wait_ge(A_t_ready, 1)
                nc.scalar.activation(decay[:, 0:SEQ], bcast_ps[:, 0:SEQ], ACT.Exp,
                                     bias=A_t[:, 0, hd_:hd_ + 1])
                nc.scalar.activation(decay[:, SEQ:SEQ + P], bcast_ps[:, P:SEQ], ACT.Exp,
                                     bias=A_t[:, 1, hd_:hd_ + 1]).then_inc(decay_ready, 1)

            def head_root_of(hd_):
                act.wait_ge(head_divided, hd_ + 1)
                inverse_root(head_root[:, :], head_sq[:, :]).then_inc(head_root_ready, 1)

            def sigmoid(p):
                c = C_MIX + 8 + p
                act.wait_ge(granules_used, G_MIX + (9 + p) * GD)
                act.wait_ge(turned, 2 * (R_Y + p))
                for t in range(TT):
                    last = nc.scalar.activation(tile[:, t, :], acc[:, TT * (c % 2) + t, :], ACT.Sigmoid,
                                                scale=rstd[:, 1, t:t + 1])
                last.then_inc(silu_ready, 1)

            def high_y(p, half):
                k = 4 * p + 2 * half
                high(R_Y + p, half, y_hi[:, k:k + 2], GAIN_HEAD + k)

            for p in range(NV):
                g = G_MIX + (8 + p) * GD
                if p:
                    head_root_of(2 * p - 2)
                    head_decay(2 * p - 1)
                split(g, 0, 3)
                if p:
                    head_root_of(2 * p - 1)
                    sigmoid(p - 1)
                else:
                    store_v(NV - 1)
                split(g, 3, 4)
                head_decay(2 * p)
                split(g, 4, 5)
                if p:
                    high_y(p - 1, 0)
                split(g, 5, 7)
                if p:
                    high_y(p - 1, 1)
                split(g, 7, 8)
            g = G_MIX_OUT
            head_root_of(HEADS - 2)
            head_decay(HEADS - 1)
            split(g, 0, 3)
            head_root_of(HEADS - 1)
            sigmoid(NV - 1)
            split(g, 3, 5)
            high_y(NV - 1, 0)
            split(g, 5, 7)
            high_y(NV - 1, 1)
            split(g, 7, 8)
            for n in range(1, ND):
                g = G_MIX_OUT + n * GD
                split(g, 0, 3)
                square(2, n - 1, R_H2 + n - 1)
                split(g, 3, 5)
                high_h(R_H2 + n - 1, n - 1, 0, GAIN_FFN[1])
                split(g, 5, 7)
                high_h(R_H2 + n - 1, n - 1, 1, GAIN_FFN[1])
                split(g, 7, 8)

            first_chunk(G_FFN[1], 2, R_H2 + ND - 1, GAIN_FFN[1])
            ffn_in(1)
            ffn_out(1)
            square(3, ND - 1, R_H3 + ND - 1)
            rms_root(3)
            last_cols = (ND - 1) * COLS
            act.wait_ge(kept, 3 * ND - 1)
            act.wait_ge(rstd_ready, 4)
            nc.scalar.activation(h[:, 0, :last_cols], h[:, 0, :last_cols], ACT.Copy,
                                 scale=rstd[:, 3, 0:1]).then_inc(act_out, 1)

        @block.vector
        def _(dve):
            steps = [0]

            def link(ins):
                steps[0] += 1
                ins.then_inc(vector_step, 1)
                dve.wait_ge(vector_step, steps[0])

            def split(g, first, last, more=0):
                for i in range(first, last):
                    n = g + i
                    dve.wait_ge(high_ready, n + 1 + more)
                    nc.vector.tensor_tensor(w_lo[:, n % RING], raw[:, n % RING],
                                            w_hi[:, n % RING].bitcast(F32), ALU.subtract)\
                        .then_inc(low_ready, 1)

            def low(r, half, hi, lo, gain=None, ps=None, more=0):
                dve.wait_ge(turned_high, 2 * r + half + 1 + 2 * more)
                ps = turn_ps if ps is None else ps
                if gain is None:
                    last = nc.vector.tensor_tensor(lo, ps[:, :].rearrange("p (k t) -> p k t", k=2),
                                                   hi.bitcast(F32), ALU.subtract)
                else:
                    for kk in range(2):
                        last = nc.vector.scalar_tensor_tensor(
                            out=lo[:, kk], in0=ps[:, kk * SEQ:(kk + 1) * SEQ],
                            scalar=gains[:, gain + kk:gain + kk + 1], in1=hi[:, kk].bitcast(F32),
                            op0=ALU.mult, op1=ALU.subtract)
                last.then_inc(turned_low, 1)

            def low_h(r, n, half, gain, ps=None):
                k = 4 * n + 2 * half
                low(r, half, u_hi[:, k:k + 2], u_lo[:, k:k + 2], gain + k, ps)

            def refine(y, x_, rough, rough_sq):
                link(nc.vector.tensor_tensor(rough_sq, rough, rough, ALU.mult))
                link(nc.vector.scalar_tensor_tensor(out=rough_sq, in0=rough_sq, scalar=-0.5, in1=x_,
                                                    op0=ALU.mult, op1=ALU.mult))
                return nc.vector.scalar_tensor_tensor(out=y, in0=rough_sq, scalar=1.5, in1=rough,
                                                      op0=ALU.add, op1=ALU.mult)

            def rms_mean(norm):
                dve.wait_ge(squared, TT * ND * (norm + 1))
                link(nc.vector.tensor_reduce(mean_sq[:, norm, :], squares[:, norm, :, :], AXX, ALU.add))
                nc.vector.tensor_scalar(mean_sq[:, norm, :], mean_sq[:, norm, :], 1.0 / D, EPS,
                                        ALU.mult, ALU.add).then_inc(mean_ready, 1)

            def rms(norm):
                dve.wait_ge(root_ready, norm + 1)
                refine(rstd[:, norm, :], mean_sq[:, norm, :], root[:, norm, :], root_sq[:, norm, :])\
                    .then_inc(rstd_ready, 1)

            def gate_hidden(i, c, g_end, r, silus, gm=0, rm=0):
                dve.wait_ge(granules_used, g_end + gm)
                dve.wait_ge(silu_ready, silus + rm)
                for t in range(TT):
                    last = nc.vector.scalar_tensor_tensor(
                        out=tile[:, t, :], in0=acc[:, TT * (c % 2) + t, :], scalar=rstd[:, 2 * i, t:t + 1],
                        in1=tile[:, t, :], op0=ALU.mult, op1=ALU.mult)
                last.then_inc(tile_ready, 1)

            def add_residual(c, g_end, r, n, factor, norm):
                dve.wait_ge(granules_used, g_end)
                dve.wait_ge(turned, 2 * min(r, R_H3))
                if n:
                    dve.wait_ge(squared, TT * (ND * norm + n))
                    dve.wait_ge(kept, ND * (norm - 1) + n)
                elif norm > 1:
                    dve.wait_ge(kept, ND * (norm - 1))
                for t in range(TT):
                    last = nc.vector.scalar_tensor_tensor(
                        out=tile[:, t, :], in0=acc[:, TT * (c % 2) + t, :], scalar=factor,
                        in1=h[:, t, n * COLS:(n + 1) * COLS], op0=ALU.mult, op1=ALU.add)
                last.then_inc(tile_ready, 1)

            def ffn_in(i):
                c, g, r = C_FFN[i], G_FFN[i], R_HID[i]
                with dve.Fori(0, NF - 1) as j:
                    split(g + GD, 0, 8 + 3, 2 * GD * j)
                    gate_hidden(i, c + 1, g + 2 * GD, r, SILUS[i] + 1, gm=2 * GD * j, rm=j)
                    split(g + 2 * GD, 3, 5, 2 * GD * j)
                    low(r, 0, g_hi[:, bass.ds(4 * j, 2)], g_lo[:, bass.ds(4 * j, 2)], more=j)
                    split(g + 2 * GD, 5, 7, 2 * GD * j)
                    low(r, 1, g_hi[:, bass.ds(4 * j + 2, 2)], g_lo[:, bass.ds(4 * j + 2, 2)], more=j)
                    split(g + 2 * GD, 7, 8, 2 * GD * j)
                split(g + (2 * NF - 1) * GD, 0, 8)

            def ffn_out(i):
                c, g, r = C_FFN_OUT[i], G_FFN_OUT[i], R_HID[i] + NF - 1
                split(g, 0, 3)
                gate_hidden(i, c - 1, g, r, SILUS[i] + NF)
                split(g, 3, 5)
                low(r, 0, g_hi[:, KF - 4:KF - 2], g_lo[:, KF - 4:KF - 2])
                split(g, 5, 7)
                low(r, 1, g_hi[:, KF - 2:KF], g_lo[:, KF - 2:KF])
                split(g, 7, GF)
                for n in range(1, ND):
                    c, g, r = c + 1, g + GF, r + 1
                    split(g, 0, 3)
                    if i == 0:
                        add_residual(c - 1, g, r, n - 1, 0.5, 1)
                        split(g, 3, 5)
                        low_h(r, n - 1, 0, GAIN_MIX)
                        split(g, 5, 7)
                        low_h(r, n - 1, 1, GAIN_MIX)
                        split(g, 7, GF)
                    else:
                        add_residual(c - 1, g, r, n - 1, 0.5, 3)
                        split(g, 3, GF)

            def first_chunk(g, c, r, gain, factor, norm):
                split(g, 0, 3)
                add_residual(c - 1, g, r, ND - 1, factor, norm)
                split(g, 3, 5)
                low_h(r, ND - 1, 0, gain)
                split(g, 5, 7)
                low_h(r, ND - 1, 1, gain)
                rms_mean(norm)
                split(g, 7, 8)
                rms(norm)

            dve.wait_ge(gains_ready, 1)
            for n in range(ND):
                for half in range(2):
                    low_h(n, n, half, GAIN_FFN[0], aux[(2 * n + half) % len(aux)])
                split(0, n, n + 1)
            rms_mean(0)
            rms(0)
            split(0, 4, 8)
            dve.wait_ge(gw_high_ready, 1)
            nc.vector.tensor_tensor(gw_lo[:, :, :], gw[:, :, :], gw_hi[:, :, :].bitcast(F32), ALU.subtract)\
                .then_inc(gw_ready, 1)
            dve.wait_ge(rstd_ready, 1)
            ffn_in(0)
            ffn_out(0)

            first_chunk(G_MIX, C_MIX, R_H1 + ND - 1, GAIN_MIX, 0.5, 1)
            dve.wait_ge(rstd_ready, 2)

            def scale_qk(n):
                c = C_MIX + n
                dve.wait_ge(granules_used, G_MIX + (n + 1) * GD)
                dve.wait_ge(turned, 2 * (R_QK + n))
                if n == 0:
                    dve.wait_ge(squared, TT * 2 * ND)
                    dve.wait_ge(kept, ND)
                for t in range(TT):
                    last = nc.vector.tensor_scalar(tile[:, t, :], acc[:, TT * (c % 2) + t, :],
                                                   rstd[:, 1, t:t + 1], None, ALU.mult)
                last.then_inc(tile_ready, 1)

            def store_qk(n, half):
                dve.wait_ge(turned_high, 2 * (R_QK + n) + half + 1)
                dst, head = (q_t, 4 * n) if n < NQ else (k_t, 4 * (n - NQ))
                nc.vector.tensor_scalar(dst[:, head + 2 * half + 1], turn_ps[:, SEQ:2 * SEQ],
                                        1.0 if n < NQ else K_SCALE, None, ALU.mult)\
                    .then_inc(turned_low, 1)

            for n in range(1, 5):
                g = G_MIX + n * GD
                split(g, 0, 1)
                if n == 2:
                    dve.wait_ge(gates_summed, 1)
                    for t in range(TT):
                        last = nc.vector.tensor_scalar(gates[:, t, :],
                                                       bcast_ps[:, t * 2 * HEADS:(t + 1) * 2 * HEADS],
                                                       rstd[:, 1, t:t + 1], None, ALU.mult)
                    last.then_inc(gates_ready, 1)
                if n == 3:
                    dve.wait_ge(gates_turned, 1)
                    dve.wait_ge(bias_landed, 16)
                    nc.vector.tensor_scalar(f_pre[:, :], scores_ps[0:HEADS, SEQ:2 * SEQ], gate_bias[:, 1:2],
                                            None, ALU.add).then_inc(f_ready, 1)
                    dve.wait_ge(f_ready, 1)
                    nc.vector.scalar_tensor_tensor(out=f_abs[:, :], in0=f_pre[:, :], scalar=-1.0,
                                                   in1=f_pre[:, :], op0=ALU.mult, op1=ALU.max)\
                        .then_inc(f_ready, 1)
                    link(nc.vector.tensor_scalar(f_pre[:, :], f_pre[:, :], 0.0, None, ALU.min))
                split(g, 1, 3)
                scale_qk(n - 1)
                if n == 3:
                    dve.wait_ge(log_ready, 1)
                    link(nc.vector.tensor_tensor_scan(B[:, :], f_pre[:, :], f_abs[:, :], 0.0,
                                                      ALU.add, ALU.subtract))
                    link(nc.vector.scalar_tensor_tensor(out=A[:, :], in0=scores_ps[0:HEADS, 0:SEQ],
                                                        scalar=gate_bias[:, 0:1], in1=B[:, :],
                                                        op0=ALU.add, op1=ALU.subtract))
                    link(nc.vector.tensor_tensor_scan(M[:, :], A[:, :], A[:, :], 0.0, ALU.max, ALU.max))
                    link(nc.vector.tensor_tensor(B[:, :], B[:, :], M[:, :], ALU.add))
                    nc.vector.tensor_scalar(M[:, :], M[:, :], -1.0, None, ALU.mult)\
                        .then_inc(stab_ready, 1)
                split(g, 3, 5)
                store_qk(n - 1, 0)
                split(g, 5, 7)
                store_qk(n - 1, 1)
                split(g, 7, 8)
            for n in range(5, 8):
                g = G_MIX + n * GD
                split(g, 0, 1)
                if n == 5:
                    dve.wait_ge(floor_ready, 1)
                    for t in range(TT):
                        last = nc.vector.tensor_copy(A_t[:, t, :],
                                                     bcast_ps[:, 2 * t * HEADS:(2 * t + 1) * HEADS])
                    last.then_inc(A_t_ready, 1)
                split(g, 1, 8)

            def head_weights(hd_):
                dve.wait_ge(decay_masked, hd_ + 1)
                if hd_:
                    dve.wait_ge(num_ready, hd_)
                nc.vector.tensor_tensor(weighted[:, :], scores_ps[:, 0:3 * P], decay[:, :], ALU.mult)\
                    .then_inc(weighted_ready, 1)

            def head_divide(hd_):
                at = hd_ % 2 * VD
                dve.wait_ge(num_ready, hd_ + 1)
                link(nc.vector.tensor_tensor(den[:, :], den_ps, floor_t[:, :, hd_], ALU.max))
                link(nc.vector.scalar_tensor_tensor(out=den[:, :], in0=den_ps, scalar=-1.0,
                                                    in1=den[:, :], op0=ALU.mult, op1=ALU.max))
                link(nc.vector.reciprocal(den_inv[:, :], den[:, :]))
                for t in range(TT):
                    last = nc.vector.tensor_scalar(heads_out[:, t, at:at + VD],
                                                   num_ps[:, t * VD:(t + 1) * VD],
                                                   den_inv[:, t:t + 1], None, ALU.mult)
                link(last)
                for t in range(TT):
                    link(nc.vector.scalar_tensor_tensor(
                        out=scratch_v[:, :], in0=heads_out[:, t, at:at + VD], scalar=1.0,
                        in1=heads_out[:, t, at:at + VD], op0=ALU.mult, op1=ALU.mult,
                        accum_out=head_sq[:, t:t + 1]))
                nc.vector.tensor_scalar(head_sq[:, :], head_sq[:, :], 1.0 / VD, EPS, ALU.mult, ALU.add)\
                    .then_inc(head_divided, 1)

            def head_norm(hd_):
                at = hd_ % 2 * VD
                dve.wait_ge(head_root_ready, hd_ + 1)
                link(refine(head_rstd[:, :], head_sq[:, :], head_root[:, :], head_root_sq[:, :]))
                for t in range(TT):
                    last = nc.vector.tensor_scalar(heads_out[:, t, at:at + VD], heads_out[:, t, at:at + VD],
                                                   head_rstd[:, t:t + 1], None, ALU.mult)
                last.then_inc(head_ready, 1)

            def gate_heads(p):
                dve.wait_ge(silu_ready, NF + p + 1)
                dve.wait_ge(head_ready, 2 * p + 2)
                nc.vector.tensor_tensor(tile[:, :, :], tile[:, :, :], heads_out[:, :, :], ALU.mult)\
                    .then_inc(tile_ready, 1)

            def low_y(p, half):
                k = 4 * p + 2 * half
                low(R_Y + p, half, y_hi[:, k:k + 2], y_lo[:, k:k + 2], GAIN_HEAD + k)

            for p in range(NV):
                g = G_MIX + (8 + p) * GD
                split(g, 0, 1)
                if p:
                    head_norm(2 * p - 2)
                    head_weights(2 * p - 1)
                split(g, 1, 3)
                if p:
                    head_divide(2 * p - 1)
                    head_norm(2 * p - 1)
                    gate_heads(p - 1)
                split(g, 3, 5)
                head_weights(2 * p)
                if p:
                    low_y(p - 1, 0)
                split(g, 5, 7)
                head_divide(2 * p)
                if p:
                    low_y(p - 1, 1)
                split(g, 7, 8)
            g = G_MIX_OUT
            split(g, 0, 1)
            head_norm(HEADS - 2)
            head_weights(HEADS - 1)
            split(g, 1, 3)
            head_divide(HEADS - 1)
            head_norm(HEADS - 1)
            gate_heads(NV - 1)
            split(g, 3, 5)
            low_y(NV - 1, 0)
            split(g, 5, 7)
            low_y(NV - 1, 1)
            split(g, 7, 8)
            for n in range(1, ND):
                g = G_MIX_OUT + n * GD
                r = R_H2 + n - 1
                split(g, 0, 3)
                add_residual(C_MIX_OUT + n - 1, g, r, n - 1, 1.0, 2)
                split(g, 3, 5)
                low_h(r, n - 1, 0, GAIN_FFN[1])
                split(g, 5, 7)
                low_h(r, n - 1, 1, GAIN_FFN[1])
                split(g, 7, 8)

            first_chunk(G_FFN[1], C_FFN[1], R_H2 + ND - 1, GAIN_FFN[1], 1.0, 2)
            dve.wait_ge(rstd_ready, 3)
            ffn_in(1)
            ffn_out(1)
            add_residual(C_FFN_OUT[1] + ND - 1, G_FFN_OUT[1] + ND * GF, R_H3 + ND - 1, ND - 1, 0.5, 3)
            last_cols = (ND - 1) * COLS
            rms_mean(3)
            rms(3)
            dve.wait_ge(rstd_ready, 4)
            for t in range(TT):
                last = nc.vector.scalar_tensor_tensor(out=tile[:, t, :], in0=tile[:, t, :],
                                                      scalar=rstd[:, 3, t:t + 1],
                                                      in1=final_gain[:, last_cols:],
                                                      op0=ALU.mult, op1=ALU.mult)
            last.then_inc(vec_out, 1)
            dve.wait_ge(kept, 3 * ND - 1)
            nc.vector.tensor_scalar(h[:, 1, :last_cols], h[:, 1, :last_cols], rstd[:, 3, 1:2], None,
                                    ALU.mult).then_inc(vec_out, 1)


_INS = ["x", "ffn_norm", "ffn_w_in", "ffn_w_out", "mix_norm", "a_w_in", "a_b_if", "a_head_norm",
        "a_w_out", "final_norm"]


def kernel(**inputs):
    import numpy as _np
    import concourse.bacc as _bacc
    from concourse import mybir as _mybir
    from concourse.bass_utils import run_bass_kernel_spmd as _run

    nc = _bacc.Bacc("TRN2", target_bir_lowering=False, num_devices=1)
    arrays, args = {}, []
    for name in _INS:
        a = _np.ascontiguousarray(inputs[name])
        arrays[f"in_{name}_dram"] = a
        args.append(nc.dram_tensor(f"in_{name}_dram", a.shape, _mybir.dt.from_np(a.dtype),
                                   kind="ExternalInput").ap())
    shape = inputs["x"].shape
    args.append(nc.dram_tensor("out_0_dram", shape, _mybir.dt.float32, kind="ExternalOutput").ap())
    trunk_program(nc, *args)
    r = _run(nc, [arrays], core_ids=[0])
    return r.results[0]["out_0_dram"]
```

```python
from contextlib import ExitStack

import concourse.bass as bass
from concourse import mybir

F32 = mybir.dt.float32
F32R = mybir.dt.float32r
I32 = mybir.dt.int32
ALU = mybir.AluOpType
ACT = mybir.ActivationFunctionType
AXX = mybir.AxisListType.X

P = 128
F_AT = 32
COLS = 512
GK = 2
RING = 4
EPS = 1e-6


def trunk_program(nc, x, ffn_norm, ffn_w_in, ffn_w_out, mix_norm, a_w_in, a_b_if, a_head_norm,
                  a_w_out, final_norm, out):
    _, SEQ, D = x.shape
    FF = ffn_w_out.shape[2]
    HEADS = a_b_if.shape[1] // 2
    QK = D // (2 * HEADS)
    VD = D // HEADS
    TT = SEQ // P
    KD, KF = D // P, FF // P
    ND, NF = D // COLS, FF // COLS
    GD, GF = KD // GK, KF // GK
    NQ, NV = HEADS * QK // COLS, HEADS * VD // COLS
    K_SCALE = QK ** -0.5
    GKT = F_AT // HEADS
    assert TT == 2 and QK == P and VD == 2 * P and GD == 8 and GD % RING == 0 and 2 * GF % RING == 0

    C_FFN = (0, 2 * NF + 2 * ND + 2 * NQ + 2 * NV)
    C_FFN_OUT = tuple(c + 2 * NF for c in C_FFN)
    C_MIX = C_FFN_OUT[0] + ND
    C_MIX_OUT = C_MIX + 2 * NQ + 2 * NV
    G_FFN = (0, 2 * NF * GD + ND * GF + (2 * NQ + 2 * NV + ND) * GD)
    G_FFN_OUT = tuple(g + 2 * NF * GD for g in G_FFN)
    G_MIX = G_FFN_OUT[0] + ND * GF
    G_MIX_OUT = G_MIX + (2 * NQ + 2 * NV) * GD
    assert C_FFN[1] == C_MIX_OUT + ND and G_FFN[1] == G_MIX_OUT + ND * GD
    R_X = 0
    R_HID1 = R_X + ND
    R_H1 = R_HID1 + NF
    R_QK = R_H1 + ND
    R_Y = R_QK + 2 * NQ
    R_H2 = R_Y + NV
    R_HID2 = R_H2 + ND
    R_H3 = R_HID2 + NF
    R_HID = (R_HID1, R_HID2)
    SILUS = (0, NF + NV)

    with ExitStack() as ctx:
        def sb(name, shape, dt=F32):
            return ctx.enter_context(nc.sbuf_tensor(name, shape, dt))

        def sem(name):
            return ctx.enter_context(nc.semaphore(name))

        h = sb("h", [P, TT, D])
        u_hi = sb("u_hi", [P, KD, SEQ], F32R)
        u_lo = sb("u_lo", [P, KD, SEQ], F32R)
        raw = sb("raw", [P, RING, GK, COLS])
        w_hi = sb("w_hi", [P, RING, GK, COLS], F32R)
        w_lo = sb("w_lo", [P, RING, GK, COLS], F32R)
        tile = sb("tile", [P, TT, COLS])
        final_gain = sb("final_gain", [P, D])
        ident = sb("ident", [P, P])
        gain_rows = sb("gain_rows", [3 * KD, P])
        first_rows = sb("first_rows", [KD, P])
        gains = sb("gains", [P, 4 * KD])
        squares = sb("squares", [P, 4, TT, ND])
        mean_sq = sb("mean_sq", [P, 4, TT])
        newton = sb("newton", [P, 4, 2 * TT])
        rstd = sb("rstd", [P, 4, TT])
        with ExitStack() as mixer_place:
            def mx(name, shape, dt=F32):
                return mixer_place.enter_context(nc.sbuf_tensor(name, shape, dt))

            y_hi = mx("y_hi", [P, KD, SEQ], F32R)
            y_lo = mx("y_lo", [P, KD, SEQ], F32R)
            q_t = mx("q_t", [P, HEADS, SEQ])
            k_t = mx("k_t", [P, HEADS, SEQ])
            v = mx("v", [P, TT, HEADS * VD])
            heads_out = mx("heads_out", [P, TT, COLS])
            rstd_row = mx("rstd_row", [P, SEQ])
            f_pre = mx("f_pre", [HEADS, SEQ])
            f_abs = mx("f_abs", [HEADS, SEQ])
            A = mx("A", [HEADS, SEQ])
            M = mx("M", [HEADS, SEQ])
            minus_M_hi = mx("minus_M_hi", [HEADS, SEQ], F32R)
            minus_M_lo = mx("minus_M_lo", [HEADS, SEQ], F32R)
            B = mx("B", [HEADS, SEQ])
            decay = mx("decay", [P, 3 * P])
            weighted = mx("weighted", [P, 3 * P])
            scratch_v = mx("scratch_v", [P, VD])
        with ExitStack() as hidden_place:
            def hd(name, shape, dt=F32):
                return hidden_place.enter_context(nc.sbuf_tensor(name, shape, dt))

            g_hi = hd("g_hi", [P, KF, SEQ], F32R)
            g_lo = hd("g_lo", [P, KF, SEQ], F32R)
        ctx.enter_context(nc.sbuf_tensor("hidden_fence", [P, 2 * KF, SEQ], F32))
        GWS = 2 * KD * HEADS + P
        gw = tile[:, 0, 0:GWS]
        gw_hi = sb("gw_hi", [P, GWS], F32R)
        gw_lo = sb("gw_lo", [P, GWS], F32R)
        gate_bias = sb("gate_bias", [HEADS, 2])
        select = sb("select", [HEADS, HEADS, P], F32R)
        ones = sb("ones", [P, 1])
        A_t = sb("A_t", [P, TT, HEADS])
        floor_t = sb("floor_t", [P, TT, HEADS])
        den = sb("den", [P, TT])
        den_inv = sb("den_inv", [P, TT])
        head_sq = sb("head_sq", [P, TT])
        head_newton = sb("head_newton", [P, 2 * TT])
        head_rstd = sb("head_rstd", [P, TT])
        scratch = sb("scratch", [P, COLS])

        acc = ctx.enter_context(nc.psum_tensor("acc", [P, 2 * TT, COLS], F32))
        aux = [ctx.enter_context(nc.psum_tensor(f"aux{i}", [P, COLS], F32)) for i in range(4)]
        bcast_ps, scores_ps, num_ps, turn_ps = aux
        den_ps = bcast_ps[:, SEQ:SEQ + TT]

        x_landed = [sem(f"x_landed{n}") for n in range(ND)]
        first_gain_landed = sem("first_gain_landed")
        gains_landed = sem("gains_landed")
        gw_landed = sem("gw_landed")
        bias_landed = sem("bias_landed")
        final_gain_landed = sem("final_gain_landed")
        raw_landed = [sem(f"raw_landed{i}") for i in range(RING)]
        high_ready = sem("high_ready")
        low_ready = sem("low_ready")
        granules_used = sem("granules_used")
        tile_ready = sem("tile_ready")
        turned = sem("turned")
        turned_high = sem("turned_high")
        turned_low = sem("turned_low")
        squared = sem("squared")
        kept = sem("kept")
        silu_ready = sem("silu_ready")
        rstd_ready = sem("rstd_ready")
        consts_ready = sem("consts_ready")
        gain_turned = sem("gain_turned")
        gains_ready = sem("gains_ready")
        gw_high_ready = sem("gw_high_ready")
        gw_ready = sem("gw_ready")
        v_ready = sem("v_ready")
        gates_summed = sem("gates_summed")
        rstd_row_ready = sem("rstd_row_ready")
        f_ready = sem("f_ready")
        exp_f = sem("exp_f")
        log_ready = sem("log_ready")
        stab_ready = sem("stab_ready")
        stab_turned = sem("stab_turned")
        A_t_ready = sem("A_t_ready")
        floor_ready = sem("floor_ready")
        scores_ready = sem("scores_ready")
        decay_ready = sem("decay_ready")
        decay_masked = sem("decay_masked")
        weighted_ready = sem("weighted_ready")
        num_ready = sem("num_ready")
        head_divided = sem("head_divided")
        head_ready = sem("head_ready")
        vector_step = sem("vector_step")
        last_summed = sem("last_summed")
        last_ready = sem("last_ready")
        act_out = sem("act_out")
        vec_out = sem("vec_out")
        out_stored = sem("out_stored")

        w_in = [ffn_w_in[0, i].rearrange("(k p) n -> p k n", p=P) for i in range(2)]
        w_out = [ffn_w_out[0, i].rearrange("(k p) n -> p k n", p=P) for i in range(2)]
        mix_in = a_w_in[0].rearrange("(k p) n -> p k n", p=P)
        mix_out = a_w_out[0].rearrange("(k p) n -> p k n", p=P)
        x_tokens = x[0].rearrange("(t p) n -> p t n", p=P)
        out_tokens = out[0].rearrange("(t p) n -> p t n", p=P)
        GAIN_FFN = (0, 2 * KD)
        GAIN_MIX, GAIN_HEAD = KD, 3 * KD

        block = ctx.enter_context(nc.Block())

        @block.sync
        def _(sp):
            def load(w, g, more, k0, col):
                if g >= RING:
                    sp.wait_ge(low_ready, g - RING + 1 + more)
                sp.dma_start(raw[:, g % RING], w[:, k0:k0 + GK, bass.ds(col, COLS)])\
                    .then_inc(raw_landed[g % RING], 16)

            def load_pair(w, g, more, col0, col1, granules):
                for i in range(granules):
                    load(w, g + i, more, GK * i, col0)
                for i in range(granules):
                    load(w, g + granules + i, more, GK * i, col1)

            for n in range(ND):
                sp.dma_start(h[:, :, n * COLS:(n + 1) * COLS], x_tokens[:, :, n * COLS:(n + 1) * COLS])\
                    .then_inc(x_landed[n], 16)
                if n < 2:
                    load(w_in[0], 2 * n, 0, GK * 2 * n, 0)
                    load(w_in[0], 2 * n + 1, 0, GK * (2 * n + 1), 0)
            for i in range(RING, GD):
                load(w_in[0], i, 0, GK * i, 0)
            for i in range(GD):
                load(w_in[0], GD + i, 0, GK * i, FF)
            with sp.Fori(0, NF - 1) as j:
                load_pair(w_in[0], G_FFN[0] + 2 * GD, 2 * GD * j, j * COLS + COLS,
                          j * COLS + (COLS + FF), GD)
            with sp.Fori(0, ND // 2) as m:
                load_pair(w_out[0], G_FFN_OUT[0], 2 * GF * m, 2 * COLS * m, 2 * COLS * m + COLS, GF)
            with sp.Fori(0, NQ + NV) as m:
                load_pair(mix_in, G_MIX, 2 * GD * m, 2 * COLS * m, 2 * COLS * m + COLS, GD)
            with sp.Fori(0, ND // 2) as m:
                load_pair(mix_out, G_MIX_OUT, 2 * GD * m, 2 * COLS * m, 2 * COLS * m + COLS, GD)
            with sp.Fori(0, NF) as j:
                load_pair(w_in[1], G_FFN[1], 2 * GD * j, j * COLS, j * COLS + FF, GD)
            with sp.Fori(0, ND // 2) as m:
                load_pair(w_out[1], G_FFN_OUT[1], 2 * GF * m, 2 * COLS * m, 2 * COLS * m + COLS, GF)

            half = D // 2
            sp.wait_ge(vec_out, 1)
            sp.dma_start(out_tokens[:, 0, :], h[:, 0, :]).then_inc(out_stored, 16)
            sp.wait_ge(vec_out, 2)
            sp.dma_start(out_tokens[:, 1, 0:half], h[:, 1, 0:half]).then_inc(out_stored, 16)
            sp.wait_ge(act_out, 1)
            sp.dma_start(out_tokens[:, 1, half:], h[:, 1, half:]).then_inc(out_stored, 16)
            sp.wait_ge(out_stored, 48)

        @block.gpsimd
        def _(pool):
            nc.gpsimd.memset(ident[:, :], 0.0).then_inc(consts_ready, 1)
            nc.gpsimd.memset(select[:, :, :].bitcast(F32), 1.0).then_inc(consts_ready, 1)
            nc.gpsimd.memset(gw[:, 2 * KD * HEADS:], 0.0)
            nc.gpsimd.memset(ones[:, :], 1.0).then_inc(consts_ready, 1)
            pool.wait_ge(consts_ready, 3)
            nc.gpsimd.affine_select(out=ident[:, :], in_=ident[:, :], compare_op=ALU.not_equal, fill=1.0,
                                    base=0, pattern=[[-1, P]], channel_multiplier=1)\
                .then_inc(consts_ready, 1)
            nc.gpsimd.affine_select(out=select[:, :, :], in_=select[:, :, :].bitcast(F32),
                                    compare_op=ALU.is_equal, fill=0.0, base=0, pattern=[[-1, HEADS], [0, P]],
                                    channel_multiplier=1).then_inc(consts_ready, 1)
            for n in range(2 * KD // GKT):
                k0, col = n // 2 * GKT, 2 * (NQ + NV) * COLS + n % 2 * HEADS
                pool.dma_start(gw[:, n * F_AT:(n + 1) * F_AT].rearrange("p (k h) -> p k h", h=HEADS),
                               mix_in[:, k0:k0 + GKT, col:col + HEADS]).then_inc(gw_landed, 16)
            pool.dma_start(gate_bias[:, :], a_b_if[0].rearrange("(a h) -> h a", a=2),
                           allow_slow_non_contiguous=True)\
                .then_inc(bias_landed, 16)
            pool.dma_start(final_gain[:, :], final_norm.partition_broadcast(P))\
                .then_inc(final_gain_landed, 16)

            def keep(r, n):
                pool.wait_ge(tile_ready, r - R_HID1 + 1)
                nc.gpsimd.tensor_copy(h[:, :, n * COLS:(n + 1) * COLS], tile[:, :, :])\
                    .then_inc(kept, 1)

            for n in range(ND):
                keep(R_H1 + n, n)

            for hd_ in range(HEADS):
                pool.wait_ge(decay_ready, hd_ + 1)
                for at in (0, 2 * P):
                    last = nc.gpsimd.affine_select(out=decay[:, at:at + P], in_=decay[:, at:at + P],
                                                   compare_op=ALU.is_ge, fill=0.0, base=0,
                                                   pattern=[[1, P]], channel_multiplier=-1)
                last.then_inc(decay_masked, 1)

            for n in range(ND):
                keep(R_H2 + n, n)
            pool.wait_ge(final_gain_landed, 16)
            for n in range(ND):
                cols = slice(n * COLS, (n + 1) * COLS)
                for t in range(TT):
                    if n == ND - 1:
                        pool.wait_ge(last_ready, t + 1)
                    elif t == 0:
                        pool.wait_ge(tile_ready, R_H3 + n - R_HID1 + 1)
                    last = nc.gpsimd.tensor_tensor(h[:, t, cols], tile[:, t, :], final_gain[:, cols],
                                                   ALU.mult)
                    if n == ND - 1 or t == TT - 1:
                        last.then_inc(kept, 1)

        @block.tensor
        def _(pe):

            def matmuls(c, ring, k, kk, t, granules, s_hi, s_lo):
                tok = slice(t * P, (t + 1) * P)
                for n, (s, w) in enumerate(((s_hi, w_hi), (s_hi, w_lo), (s_lo, w_hi))):
                    mm = nc.tensor.matmul(acc[:, TT * (c % 2) + t, :], s[:, k, tok], w[:, ring, kk, :],
                                          start=(k == 0 and n == 0),
                                          stop=(k == GK * granules - 1 and n == 2))
                return mm

            def run(c, g, more, first, last, granules, s_hi, s_lo, need=None):
                for i in range(first, last):
                    if need is not None:
                        pe.wait_ge(turned_low, 2 * need + i + 1)
                    pe.wait_ge(low_ready, g + i + 1 + more)
                    ring = (g + i) % RING
                    for kk in range(GK):
                        for t in range(TT):
                            mm = matmuls(c, ring, GK * i + kk, kk, t, granules, s_hi, s_lo)
                    mm.then_inc(granules_used, 1)

            def turn(r, more, half, src=None, ps=None):
                if half == 0 and src is None:
                    pe.wait_ge(tile_ready, r - R_HID1 + 1 + more)
                if ps is None:
                    pe.wait_ge(turned_low, 2 * r + half + more * 2)
                    ps = turn_ps
                for kk in range(2):
                    for t in range(TT):
                        a, at = (2 * half + kk) * P, kk * SEQ + t * P
                        block_ = tile[:, t, a:a + P] if src is None else h[:, t, src + a:src + a + P]
                        mm = nc.tensor.transpose(ps[:, at:at + P], block_, ident[:, :])
                mm.then_inc(turned, 1)

            def chunk_turn(c, g, granules, s_hi, s_lo, r, gm=0, rm=0, wait_from=None):
                run(c, g, gm, 0, 2, granules, s_hi, s_lo)
                turn(r, rm, 0)
                run(c, g, gm, 2, 4, granules, s_hi, s_lo)
                turn(r, rm, 1)
                if wait_from is None:
                    run(c, g, gm, 4, granules, granules, s_hi, s_lo)
                else:
                    run(c, g, gm, 4, wait_from, granules, s_hi, s_lo)
                    pe.wait_ge(turned_low, 2 * r + 1 + 2 * rm)
                    run(c, g, gm, wait_from, wait_from + 1, granules, s_hi, s_lo)
                    pe.wait_ge(turned_low, 2 * r + 2 + 2 * rm)
                    run(c, g, gm, wait_from + 1, granules, granules, s_hi, s_lo)

            def ffn_out_turned():
                pe.wait_ge(silu_ready, NF)
                with pe.Fori(0, ND // 2) as m:
                    chunk_turn(C_FFN_OUT[0], G_FFN_OUT[0], GF, g_hi, g_lo, R_HID1 + NF - 1,
                               gm=2 * GF * m, rm=2 * m, wait_from=GF - 2)
                    chunk_turn(C_FFN_OUT[0] + 1, G_FFN_OUT[0] + GF, GF, g_hi, g_lo, R_HID1 + NF,
                               gm=2 * GF * m, rm=2 * m)

            def ffn_out_last():
                c, g = C_FFN_OUT[1], G_FFN_OUT[1]
                pe.wait_ge(silu_ready, 2 * NF + NV)
                chunk_turn(c, g, GF, g_hi, g_lo, R_HID2 + NF - 1, wait_from=GF - 2)
                for n in range(1, ND):
                    if n >= 2:
                        pe.wait_ge(tile_ready, R_H3 + n - 2 - R_HID1 + 1)
                    run(c + n, g + n * GF, 0, 0, GF if n < ND - 1 else GF - RING, GF, g_hi, g_lo)
                g += (ND - 1) * GF
                for t in range(TT):
                    for i in range(GF - RING, GF):
                        if t == 0:
                            pe.wait_ge(low_ready, g + i + 1)
                        for kk in range(GK):
                            mm = matmuls(c + ND - 1, (g + i) % RING, GK * i + kk, kk, t, GF, g_hi, g_lo)
                    mm.then_inc(last_summed, 1)

            def ffn_in_rest(i):
                c, g, r = C_FFN[i], G_FFN[i], R_HID[i]
                with pe.Fori(0, NF - 1) as j:
                    run(c + 1, g + GD, 2 * GD * j, 0, GD, GD, u_hi, u_lo)
                    pe.wait_ge(silu_ready, SILUS[i] + 1 + j)
                    chunk_turn(c + 2, g + 2 * GD, GD, u_hi, u_lo, r, gm=2 * GD * j, rm=j)
                run(c + 2 * NF - 1, g + (2 * NF - 1) * GD, 0, 0, GD, GD, u_hi, u_lo)

            pe.wait_ge(consts_ready, 4)
            pe.wait_ge(first_gain_landed, 16)
            nc.tensor.transpose(acc[:, 0, 0:KD], first_rows[:, :], ident[0:KD, 0:KD])\
                .then_inc(gain_turned, 1)

            def turn_x(n):
                pe.wait_ge(x_landed[n], 16)
                for half in range(2):
                    q = 2 * n + half
                    if q >= len(aux):
                        pe.wait_ge(turned_low, q - len(aux) + 1)
                    turn(n, 0, half, src=n * COLS, ps=aux[q % len(aux)])

            turn_x(0)
            pe.wait_ge(gains_ready, 1)
            turn_x(1)
            run(C_FFN[0], G_FFN[0], 0, 0, 1, GD, u_hi, u_lo, need=R_X)
            turn_x(2)
            run(C_FFN[0], G_FFN[0], 0, 1, 2, GD, u_hi, u_lo, need=R_X)
            turn_x(3)
            run(C_FFN[0], G_FFN[0], 0, 2, 6, GD, u_hi, u_lo, need=R_X)
            pe.wait_ge(gains_landed, 48)
            pe.wait_ge(turned_low, 2 * ND)
            nc.tensor.transpose(bcast_ps[:, 0:3 * KD], gain_rows[:, :], ident[0:3 * KD, 0:3 * KD])\
                .then_inc(gain_turned, 1)
            run(C_FFN[0], G_FFN[0], 0, 6, GD, GD, u_hi, u_lo, need=R_X)
            ffn_in_rest(0)
            ffn_out_turned()

            def mix(n):
                return C_MIX + n, G_MIX + n * GD

            c, g = mix(0)
            chunk_turn(c, g, GD, u_hi, u_lo, R_H1 + ND - 1, wait_from=GD - 2)
            c, g = mix(1)
            run(c, g, 0, 0, 2, GD, u_hi, u_lo)
            turn(R_QK, 0, 0)
            run(c, g, 0, 2, 4, GD, u_hi, u_lo)
            turn(R_QK, 0, 1)
            run(c, g, 0, 4, 6, GD, u_hi, u_lo)
            pe.wait_ge(gw_ready, 1)
            for k in range(KD):
                for n, (w, s) in enumerate(((gw_hi, u_hi), (gw_hi, u_lo), (gw_lo, u_hi))):
                    at = k // GKT * 2 * F_AT + k % GKT * HEADS
                    nc.tensor.matmul(scores_ps[:, 0:SEQ], w[:, at:at + P], s[:, k, :],
                                     start=(k == 0 and n == 0), stop=(k == KD - 1 and n == 2))
            pe.wait_ge(rstd_ready, 2)
            for t in range(TT):
                mm = nc.tensor.transpose(bcast_ps[:, t * P:(t + 1) * P],
                                         rstd[:, 1, t:t + 1].to_broadcast([P, P]), ident[:, :])
            mm.then_inc(gates_summed, 1)
            run(c, g, 0, 6, GD, GD, u_hi, u_lo)
            c, g = mix(2)
            chunk_turn(c, g, GD, u_hi, u_lo, R_QK + 1)
            c, g = mix(3)
            chunk_turn(c, g, GD, u_hi, u_lo, R_QK + 2)
            pe.wait_ge(stab_ready, 1)
            for a, row in enumerate((A, B)):
                for t in range(TT):
                    mm = nc.tensor.transpose(bcast_ps[:, (t * 2 + a) * HEADS:(t * 2 + a + 1) * HEADS],
                                             row[:, t * P:(t + 1) * P], ident[0:HEADS, 0:HEADS])
            mm.then_inc(stab_turned, 1)
            c, g = mix(4)
            chunk_turn(c, g, GD, u_hi, u_lo, R_QK + 3)
            for n in range(5, 8):
                c, g = mix(n)
                if n >= 6:
                    pe.wait_ge(v_ready, n - 5)
                run(c, g, 0, 0, GD, GD, u_hi, u_lo)

            def head_scores(hd_):
                if hd_ == 0:
                    pe.wait_ge(A_t_ready, 1)
                    pe.wait_ge(floor_ready, 1)
                else:
                    pe.wait_ge(head_divided, hd_)
                for n, part in enumerate((minus_M_hi, minus_M_lo)):
                    nc.tensor.matmul(bcast_ps[:, 0:SEQ], select[:, hd_, :], part[:, :],
                                     start=n == 0, stop=n == 1)
                nc.tensor.matmul(scores_ps[:, 0:SEQ], k_t[:, hd_, 0:P], q_t[:, hd_, :],
                                 start=True, stop=True)
                nc.tensor.matmul(scores_ps[:, SEQ:SEQ + P], k_t[:, hd_, P:SEQ], q_t[:, hd_, P:SEQ],
                                 start=True, stop=True).then_inc(scores_ready, 1)

            def head_sums(hd_):
                pe.wait_ge(weighted_ready, hd_ + 1)
                cols = slice(hd_ * VD, (hd_ + 1) * VD)
                for t, parts in ((0, ((0, 0),)), (1, ((P, 0), (2 * P, 1)))):
                    for n, (at, s) in enumerate(parts):
                        first, last = n == 0, n == len(parts) - 1
                        nc.tensor.matmul(num_ps[:, t * VD:(t + 1) * VD], weighted[:, at:at + P],
                                         v[:, s, cols], start=first, stop=last)
                        mm = nc.tensor.matmul(den_ps[:, t:t + 1], weighted[:, at:at + P], ones[:, :],
                                              start=first, stop=last)
                mm.then_inc(num_ready, 1)

            for p in range(NV):
                c, g = mix(8 + p)
                if p < 2:
                    pe.wait_ge(v_ready, NV - 1 + p)
                run(c, g, 0, 0, 1, GD, u_hi, u_lo)
                head_scores(2 * p)
                run(c, g, 0, 1, 2, GD, u_hi, u_lo)
                if p:
                    turn(R_Y + p - 1, 0, 0)
                run(c, g, 0, 2, 3, GD, u_hi, u_lo)
                if p == 0:
                    pe.wait_ge(v_ready, NV)
                head_sums(2 * p)
                run(c, g, 0, 3, 4, GD, u_hi, u_lo)
                if p:
                    turn(R_Y + p - 1, 0, 1)
                run(c, g, 0, 4, 5, GD, u_hi, u_lo)
                head_scores(2 * p + 1)
                run(c, g, 0, 5, 7, GD, u_hi, u_lo)
                head_sums(2 * p + 1)
                run(c, g, 0, 7, 8, GD, u_hi, u_lo)
            with pe.Fori(0, ND // 2) as m:
                chunk_turn(C_MIX_OUT, G_MIX_OUT, GD, y_hi, y_lo, R_Y + NV - 1,
                           gm=2 * GD * m, rm=2 * m, wait_from=GD - 2)
                chunk_turn(C_MIX_OUT + 1, G_MIX_OUT + GD, GD, y_hi, y_lo, R_Y + NV,
                           gm=2 * GD * m, rm=2 * m)

            chunk_turn(C_FFN[1], G_FFN[1], GD, u_hi, u_lo, R_H2 + ND - 1, wait_from=GD - 2)
            ffn_in_rest(1)
            ffn_out_last()

        @block.scalar
        def _(act):
            def split(g, first, last, more=0):
                for i in range(first, last):
                    n = g + i
                    act.wait_ge(raw_landed[n % RING], 16 * (n // RING + 1) + 16 // RING * more)
                    if n >= RING:
                        act.wait_ge(granules_used, n - RING + 1 + more)
                    nc.scalar.activation(w_hi[:, n % RING], raw[:, n % RING], ACT.Copy)\
                        .then_inc(high_ready, 1)

            def split_rest(g, first):
                steps = (GF - first) // RING
                with act.Fori(0, steps) as q:
                    split(g + first, 0, RING, RING * q)
                split(g, first + steps * RING, GF)

            def high(r, half, dst, gain=None, ps=None, more=0):
                act.wait_ge(turned, 2 * r + half + 1 + 2 * more)
                ps = turn_ps if ps is None else ps
                if gain is None:
                    last = nc.scalar.activation(dst, ps[:, :].rearrange("p (k t) -> p k t", k=2), ACT.Copy)
                else:
                    for kk in range(2):
                        last = nc.scalar.activation(dst[:, kk], ps[:, kk * SEQ:(kk + 1) * SEQ], ACT.Copy,
                                                    scale=gains[:, gain + kk:gain + kk + 1])
                last.then_inc(turned_high, 1)

            def high_h(r, n, half, gain, ps=None):
                k = 4 * n + 2 * half
                high(r, half, u_hi[:, k:k + 2], gain + k, ps)

            def square(norm, n, r):
                if r is None:
                    act.wait_ge(x_landed[n], 16)
                elif r < R_H3 + ND - 1:
                    act.wait_ge(tile_ready, r - R_HID1 + 1)
                for t in range(TT):
                    if r == R_H3 + ND - 1:
                        act.wait_ge(last_ready, t + 1)
                    src = h[:, t, n * COLS:(n + 1) * COLS] if r is None else tile[:, t, :]
                    done = TT * (ND * norm + n) + t
                    if done:
                        act.wait_ge(squared, done)
                    nc.scalar.activation(scratch[:, :], src, ACT.Square,
                                         accum_out=squares[:, norm, t, n:n + 1]).then_inc(squared, 1)

            def silu(i, c, g_end, r, gm=0, rm=0):
                act.wait_ge(granules_used, g_end + gm)
                act.wait_ge(turned, 2 * r + 2 * rm)
                for t in range(TT):
                    last = nc.scalar.activation(tile[:, t, :], acc[:, TT * (c % 2) + t, :], ACT.Silu,
                                                scale=rstd[:, 2 * i, t:t + 1])
                last.then_inc(silu_ready, 1)

            def ffn_in(i):
                c, g, r = C_FFN[i], G_FFN[i], R_HID[i]
                act.wait_ge(rstd_ready, 2 * i + 1)
                if i:
                    act.wait_ge(kept, 2 * ND)
                else:
                    act.wait_ge(gw_ready, 1)
                with act.Fori(0, NF - 1) as j:
                    split(g + GD, 2, 3, 2 * GD * j)
                    silu(i, c, g + GD, r, gm=2 * GD * j, rm=j)
                    split(g + GD, 3, 8 + 5, 2 * GD * j)
                    high(r, 0, g_hi[:, bass.ds(4 * j, 2)], more=j)
                    split(g + 2 * GD, 5, 7, 2 * GD * j)
                    high(r, 1, g_hi[:, bass.ds(4 * j + 2, 2)], more=j)
                    split(g + 2 * GD, 7, 8 + 2, 2 * GD * j)
                g_b = g + (2 * NF - 1) * GD
                split(g_b, 2, 3)
                silu(i, c, g_b, r + NF - 1)
                split(g_b, 3, 8)

            def ffn_out(i):
                g, r = G_FFN_OUT[i], R_HID[i] + NF - 1
                split(g, 0, 5)
                high(r, 0, g_hi[:, KF - 4:KF - 2])
                split(g, 5, 7)
                high(r, 1, g_hi[:, KF - 2:KF])
                split_rest(g, 7)
                for n in range(1, ND):
                    g, r = g + GF, r + 1
                    split(g, 0, 3)
                    square(2 * i + 1, n - 1, r)
                    if i == 0:
                        split(g, 3, 5)
                        high_h(r, n - 1, 0, GAIN_MIX)
                        split(g, 5, 7)
                        high_h(r, n - 1, 1, GAIN_MIX)
                        split_rest(g, 7)
                    else:
                        split_rest(g, 3)

            def first_chunk(g, norm, r, gain):
                split(g, 0, 3)
                square(norm, ND - 1, r)
                split(g, 3, 5)
                high_h(r, ND - 1, 0, gain)
                split(g, 5, 7)
                high_h(r, ND - 1, 1, gain)
                split(g, 7, 8)

            act.dma_start(first_rows[:, :], ffn_norm[0, 0].rearrange("(k p) -> k p", p=P))\
                .then_inc(first_gain_landed, 16)
            for n, vector in enumerate((mix_norm[0], ffn_norm[0, 1], a_head_norm[0])):
                act.dma_start(gain_rows[n * KD:(n + 1) * KD, :], vector.rearrange("(k p) -> k p", p=P))\
                    .then_inc(gains_landed, 16)
            act.wait_ge(gain_turned, 1)
            nc.scalar.activation(gains[:, 0:KD], acc[:, 0, 0:KD], ACT.Copy).then_inc(gains_ready, 1)
            act.wait_ge(gains_ready, 1)
            for n in range(ND):
                for half in range(2):
                    high_h(n, n, half, GAIN_FFN[0], aux[(2 * n + half) % len(aux)])
                if n < 2:
                    split(0, 2 * n, 2 * n + 2)
            for n in range(ND):
                split(0, 4 + n, 5 + n)
                square(0, n, None)
            split(0, 8, 10)
            act.wait_ge(gain_turned, 2)
            nc.scalar.activation(gains[:, KD:], bcast_ps[:, 0:3 * KD], ACT.Copy)
            act.wait_ge(gw_landed, 16 * 2 * KD // GKT)
            nc.scalar.activation(gw_hi[:, :], gw[:, :], ACT.Copy).then_inc(gw_high_ready, 1)
            ffn_in(0)
            ffn_out(0)

            def store_qk(n, half):
                act.wait_ge(turned, 2 * (R_QK + n) + half + 1)
                dst, head = (q_t, 4 * n) if n < NQ else (k_t, 4 * (n - NQ))
                nc.scalar.activation(dst[:, head + 2 * half], turn_ps[:, 0:SEQ], ACT.Copy,
                                     scale=1.0 if n < NQ else K_SCALE).then_inc(turned_high, 1)

            first_chunk(G_MIX, 1, R_H1 + ND - 1, GAIN_MIX)
            for n in range(1, 5):
                g = G_MIX + n * GD
                split(g, 0, 1)
                if n == 2:
                    act.wait_ge(gates_summed, 1)
                    nc.scalar.activation(rstd_row[:, :], bcast_ps[:, 0:SEQ], ACT.Copy)\
                        .then_inc(rstd_row_ready, 1)
                if n == 4:
                    act.wait_ge(stab_turned, 1)
                    for t in range(TT):
                        at = (2 * t + 1) * HEADS
                        last = nc.scalar.activation(floor_t[:, t, :], bcast_ps[:, at:at + HEADS], ACT.Exp,
                                                    scale=-1.0)
                    last.then_inc(floor_ready, 1)
                split(g, 1, 3)
                if n == 2:
                    act.wait_ge(f_ready, 3)
                    nc.scalar.activation(f_abs[:, :], f_abs[:, :], ACT.Exp, scale=-1.0).then_inc(exp_f, 1)
                    act.wait_ge(exp_f, 1)
                    nc.scalar.activation(f_abs[:, :], f_abs[:, :], ACT.Ln, bias=1.0).then_inc(log_ready, 1)
                split(g, 3, 5)
                store_qk(n - 1, 0)
                split(g, 5, 7)
                store_qk(n - 1, 1)
                split(g, 7, 8)

            act.wait_ge(rstd_ready, 2)

            def store_v(n):
                g_end = G_MIX + (5 + n) * GD
                act.wait_ge(granules_used, g_end)
                for t in range(TT):
                    last = nc.scalar.activation(v[:, t, n * COLS:(n + 1) * COLS],
                                                acc[:, TT * ((C_MIX + 4 + n) % 2) + t, :], ACT.Copy,
                                                scale=rstd[:, 1, t:t + 1])
                last.then_inc(v_ready, 1)

            for n in range(5, 8):
                g = G_MIX + n * GD
                split(g, 0, 3)
                store_v(n - 5)
                split(g, 3, 8)

            def head_decay(hd_):
                act.wait_ge(scores_ready, hd_ + 1)
                if hd_:
                    act.wait_ge(weighted_ready, hd_)
                else:
                    act.wait_ge(A_t_ready, 1)
                nc.scalar.activation(decay[:, 0:SEQ], bcast_ps[:, 0:SEQ], ACT.Exp,
                                     bias=A_t[:, 0, hd_:hd_ + 1])
                nc.scalar.activation(decay[:, SEQ:SEQ + P], bcast_ps[:, P:SEQ], ACT.Exp,
                                     bias=A_t[:, 1, hd_:hd_ + 1]).then_inc(decay_ready, 1)

            def sigmoid(p):
                c = C_MIX + 8 + p
                act.wait_ge(granules_used, G_MIX + (9 + p) * GD)
                act.wait_ge(turned, 2 * (R_Y + p))
                for t in range(TT):
                    last = nc.scalar.activation(tile[:, t, :], acc[:, TT * (c % 2) + t, :], ACT.Sigmoid,
                                                scale=rstd[:, 1, t:t + 1])
                last.then_inc(silu_ready, 1)

            def high_y(p, half):
                k = 4 * p + 2 * half
                high(R_Y + p, half, y_hi[:, k:k + 2], GAIN_HEAD + k)

            for p in range(NV):
                g = G_MIX + (8 + p) * GD
                if p:
                    head_decay(2 * p - 1)
                split(g, 0, 3)
                if p:
                    sigmoid(p - 1)
                else:
                    store_v(NV - 1)
                split(g, 3, 4)
                head_decay(2 * p)
                split(g, 4, 5)
                if p:
                    high_y(p - 1, 0)
                split(g, 5, 7)
                if p:
                    high_y(p - 1, 1)
                split(g, 7, 8)
            g = G_MIX_OUT
            head_decay(HEADS - 1)
            split(g, 0, 3)
            sigmoid(NV - 1)
            split(g, 3, 5)
            high_y(NV - 1, 0)
            split(g, 5, 7)
            high_y(NV - 1, 1)
            split(g, 7, 8)
            for n in range(1, ND):
                g = G_MIX_OUT + n * GD
                split(g, 0, 3)
                square(2, n - 1, R_H2 + n - 1)
                split(g, 3, 5)
                high_h(R_H2 + n - 1, n - 1, 0, GAIN_FFN[1])
                split(g, 5, 7)
                high_h(R_H2 + n - 1, n - 1, 1, GAIN_FFN[1])
                split(g, 7, 8)

            first_chunk(G_FFN[1], 2, R_H2 + ND - 1, GAIN_FFN[1])
            split(G_FFN[1], 8, 10)
            ffn_in(1)
            ffn_out(1)
            square(3, ND - 1, R_H3 + ND - 1)
            act.wait_ge(rstd_ready, 5)
            act.wait_ge(kept, 3 * ND + 1)
            nc.scalar.activation(h[:, 1, D // 2:], h[:, 1, D // 2:], ACT.Copy, scale=rstd[:, 3, 1:2])\
                .then_inc(act_out, 1)

        @block.vector
        def _(dve):
            steps = [0]

            def link(ins):
                steps[0] += 1
                ins.then_inc(vector_step, 1)
                dve.wait_ge(vector_step, steps[0])

            def split(g, first, last, more=0):
                for i in range(first, last):
                    n = g + i
                    dve.wait_ge(high_ready, n + 1 + more)
                    nc.vector.tensor_tensor(w_lo[:, n % RING], raw[:, n % RING],
                                            w_hi[:, n % RING].bitcast(F32), ALU.subtract)\
                        .then_inc(low_ready, 1)

            def split_rest(g, first):
                rings = (GF - first) // RING
                with dve.Fori(0, rings) as q:
                    split(g + first, 0, RING, RING * q)
                split(g, first + rings * RING, GF)

            def low(r, half, hi, lo, gain=None, ps=None, more=0):
                dve.wait_ge(turned_high, 2 * r + half + 1 + 2 * more)
                ps = turn_ps if ps is None else ps
                if gain is None:
                    last = nc.vector.tensor_tensor(lo, ps[:, :].rearrange("p (k t) -> p k t", k=2),
                                                   hi.bitcast(F32), ALU.subtract)
                else:
                    for kk in range(2):
                        last = nc.vector.scalar_tensor_tensor(
                            out=lo[:, kk], in0=ps[:, kk * SEQ:(kk + 1) * SEQ],
                            scalar=gains[:, gain + kk:gain + kk + 1], in1=hi[:, kk].bitcast(F32),
                            op0=ALU.mult, op1=ALU.subtract)
                last.then_inc(turned_low, 1)

            def low_h(r, n, half, gain, ps=None):
                k = 4 * n + 2 * half
                low(r, half, u_hi[:, k:k + 2], u_lo[:, k:k + 2], gain + k, ps)

            def inverse_root(y, x_, half_):
                bits, n = y.bitcast(I32), y.shape[1]
                minus_half, term = half_[:, 0:n], half_[:, n:2 * n]
                nc.vector.tensor_scalar(minus_half, x_, -0.5, None, ALU.mult)
                link(nc.vector.tensor_scalar(bits, x_.bitcast(I32), 1, None, ALU.logical_shift_right))
                link(nc.vector.tensor_scalar(bits, bits, -1.0, float(0x5F3759DF), ALU.mult, ALU.add))
                for step in range(3):
                    for t in range(n):
                        last = nc.vector.scalar_tensor_tensor(
                            out=term[:, t:t + 1], in0=y[:, t:t + 1], scalar=minus_half[:, t:t + 1],
                            in1=y[:, t:t + 1], op0=ALU.mult, op1=ALU.mult)
                    link(last)
                    last = nc.vector.scalar_tensor_tensor(out=y, in0=term, scalar=1.5, in1=y,
                                                          op0=ALU.add, op1=ALU.mult)
                    if step < 2:
                        link(last)
                return last

            def rms(norm, t0=0, t1=TT):
                dve.wait_ge(squared, TT * ND * (norm + 1) - TT + t1)
                link(nc.vector.tensor_reduce(mean_sq[:, norm, t0:t1], squares[:, norm, t0:t1, :], AXX,
                                             ALU.add))
                link(nc.vector.tensor_scalar(mean_sq[:, norm, t0:t1], mean_sq[:, norm, t0:t1], 1.0 / D,
                                             EPS, ALU.mult, ALU.add))
                inverse_root(rstd[:, norm, t0:t1], mean_sq[:, norm, t0:t1], newton[:, norm, 2 * t0:2 * t1])\
                    .then_inc(rstd_ready, 1)

            def gate_hidden(i, c, g_end, r, silus, gm=0, rm=0):
                dve.wait_ge(granules_used, g_end + gm)
                dve.wait_ge(silu_ready, silus + rm)
                for t in range(TT):
                    last = nc.vector.scalar_tensor_tensor(
                        out=tile[:, t, :], in0=acc[:, TT * (c % 2) + t, :], scalar=rstd[:, 2 * i, t:t + 1],
                        in1=tile[:, t, :], op0=ALU.mult, op1=ALU.mult)
                last.then_inc(tile_ready, 1)

            def add_residual(c, g_end, r, n, factor, norm):
                dve.wait_ge(granules_used, g_end)
                dve.wait_ge(turned, 2 * min(r, R_H3))
                if n:
                    dve.wait_ge(squared, TT * (ND * norm + n))
                    dve.wait_ge(kept, ND * (norm - 1) + n)
                elif norm > 1:
                    dve.wait_ge(kept, ND * (norm - 1))
                for t in range(TT):
                    last = nc.vector.scalar_tensor_tensor(
                        out=tile[:, t, :], in0=acc[:, TT * (c % 2) + t, :], scalar=factor,
                        in1=h[:, t, n * COLS:(n + 1) * COLS], op0=ALU.mult, op1=ALU.add)
                last.then_inc(tile_ready, 1)

            def ffn_in(i):
                c, g, r = C_FFN[i], G_FFN[i], R_HID[i]
                with dve.Fori(0, NF - 1) as j:
                    split(g + GD, 2, 8 + 3, 2 * GD * j)
                    gate_hidden(i, c + 1, g + 2 * GD, r, SILUS[i] + 1, gm=2 * GD * j, rm=j)
                    split(g + 2 * GD, 3, 5, 2 * GD * j)
                    low(r, 0, g_hi[:, bass.ds(4 * j, 2)], g_lo[:, bass.ds(4 * j, 2)], more=j)
                    split(g + 2 * GD, 5, 7, 2 * GD * j)
                    low(r, 1, g_hi[:, bass.ds(4 * j + 2, 2)], g_lo[:, bass.ds(4 * j + 2, 2)], more=j)
                    split(g + 2 * GD, 7, 8 + 2, 2 * GD * j)
                split(g + (2 * NF - 1) * GD, 2, 8)

            def ffn_out(i):
                c, g, r = C_FFN_OUT[i], G_FFN_OUT[i], R_HID[i] + NF - 1
                split(g, 0, 3)
                gate_hidden(i, c - 1, g, r, SILUS[i] + NF)
                split(g, 3, 5)
                low(r, 0, g_hi[:, KF - 4:KF - 2], g_lo[:, KF - 4:KF - 2])
                split(g, 5, 7)
                low(r, 1, g_hi[:, KF - 2:KF], g_lo[:, KF - 2:KF])
                split_rest(g, 7)
                for n in range(1, ND):
                    c, g, r = c + 1, g + GF, r + 1
                    split(g, 0, 3)
                    if i == 0:
                        add_residual(c - 1, g, r, n - 1, 0.5, 1)
                        split(g, 3, 5)
                        low_h(r, n - 1, 0, GAIN_MIX)
                        split(g, 5, 7)
                        low_h(r, n - 1, 1, GAIN_MIX)
                        split_rest(g, 7)
                    else:
                        add_residual(c - 1, g, r, n - 1, 0.5, 3)
                        split_rest(g, 3)

            def first_chunk(g, c, r, gain, factor, norm):
                split(g, 0, 3)
                add_residual(c - 1, g, r, ND - 1, factor, norm)
                split(g, 3, 5)
                low_h(r, ND - 1, 0, gain)
                split(g, 5, 7)
                low_h(r, ND - 1, 1, gain)
                split(g, 7, 8)
                rms(norm)

            dve.wait_ge(gains_ready, 1)
            for n in range(ND):
                for half in range(2):
                    low_h(n, n, half, GAIN_FFN[0], aux[(2 * n + half) % len(aux)])
                if n < 2:
                    split(0, 2 * n, 2 * n + 2)
            split(0, 4, 8)
            rms(0)
            split(0, 8, 10)
            dve.wait_ge(gw_high_ready, 1)
            nc.vector.tensor_tensor(gw_lo[:, :], gw[:, :], gw_hi[:, :].bitcast(F32), ALU.subtract)\
                .then_inc(gw_ready, 1)
            dve.wait_ge(rstd_ready, 1)
            ffn_in(0)
            ffn_out(0)

            first_chunk(G_MIX, C_MIX, R_H1 + ND - 1, GAIN_MIX, 0.5, 1)
            dve.wait_ge(rstd_ready, 2)

            def scale_qk(n):
                c = C_MIX + n
                dve.wait_ge(granules_used, G_MIX + (n + 1) * GD)
                dve.wait_ge(turned, 2 * (R_QK + n))
                if n == 0:
                    dve.wait_ge(squared, TT * 2 * ND)
                    dve.wait_ge(kept, ND)
                for t in range(TT):
                    last = nc.vector.tensor_scalar(tile[:, t, :], acc[:, TT * (c % 2) + t, :],
                                                   rstd[:, 1, t:t + 1], None, ALU.mult)
                last.then_inc(tile_ready, 1)

            def store_qk(n, half):
                dve.wait_ge(turned_high, 2 * (R_QK + n) + half + 1)
                dst, head = (q_t, 4 * n) if n < NQ else (k_t, 4 * (n - NQ))
                nc.vector.tensor_scalar(dst[:, head + 2 * half + 1], turn_ps[:, SEQ:2 * SEQ],
                                        1.0 if n < NQ else K_SCALE, None, ALU.mult)\
                    .then_inc(turned_low, 1)

            for n in range(1, 5):
                g = G_MIX + n * GD
                split(g, 0, 1)
                if n == 2:
                    dve.wait_ge(rstd_row_ready, 1)
                    dve.wait_ge(bias_landed, 16)
                    nc.vector.tensor_tensor(A[:, :], scores_ps[0:HEADS, 0:SEQ], rstd_row[0:HEADS, :],
                                            ALU.mult)
                    nc.vector.tensor_tensor(f_pre[:, :], scores_ps[F_AT:F_AT + HEADS, 0:SEQ],
                                            rstd_row[F_AT:F_AT + HEADS, :], ALU.mult).then_inc(f_ready, 1)
                    dve.wait_ge(f_ready, 1)
                    nc.vector.tensor_scalar(f_pre[:, :], f_pre[:, :], gate_bias[:, 1:2], None, ALU.add)\
                        .then_inc(f_ready, 1)
                    dve.wait_ge(f_ready, 2)
                    nc.vector.scalar_tensor_tensor(out=f_abs[:, :], in0=f_pre[:, :], scalar=-1.0,
                                                   in1=f_pre[:, :], op0=ALU.mult, op1=ALU.max)\
                        .then_inc(f_ready, 1)
                    link(nc.vector.tensor_scalar(f_pre[:, :], f_pre[:, :], 0.0, None, ALU.min))
                if n == 4:
                    dve.wait_ge(floor_ready, 1)
                    for t in range(TT):
                        last = nc.vector.tensor_copy(A_t[:, t, :],
                                                     bcast_ps[:, 2 * t * HEADS:(2 * t + 1) * HEADS])
                    last.then_inc(A_t_ready, 1)
                split(g, 1, 3)
                scale_qk(n - 1)
                if n == 2:
                    dve.wait_ge(log_ready, 1)
                    link(nc.vector.tensor_tensor_scan(B[:, :], f_pre[:, :], f_abs[:, :], 0.0,
                                                      ALU.add, ALU.subtract))
                    link(nc.vector.scalar_tensor_tensor(out=A[:, :], in0=A[:, :],
                                                        scalar=gate_bias[:, 0:1], in1=B[:, :],
                                                        op0=ALU.add, op1=ALU.subtract))
                    link(nc.vector.tensor_tensor_scan(M[:, :], A[:, :], A[:, :], 0.0, ALU.max, ALU.max))
                    link(nc.vector.tensor_tensor(B[:, :], B[:, :], M[:, :], ALU.add))
                    link(nc.vector.tensor_scalar(minus_M_hi[:, :], M[:, :], -1.0, None, ALU.mult))
                    nc.vector.scalar_tensor_tensor(out=minus_M_lo[:, :], in0=M[:, :], scalar=-1.0,
                                                   in1=minus_M_hi[:, :].bitcast(F32), op0=ALU.mult,
                                                   op1=ALU.subtract).then_inc(stab_ready, 1)
                split(g, 3, 5)
                store_qk(n - 1, 0)
                split(g, 5, 7)
                store_qk(n - 1, 1)
                split(g, 7, 8)
            for n in range(5, 8):
                g = G_MIX + n * GD
                split(g, 0, 8)

            def head_weights(hd_):
                dve.wait_ge(decay_masked, hd_ + 1)
                if hd_:
                    dve.wait_ge(num_ready, hd_)
                nc.vector.tensor_tensor(weighted[:, :], scores_ps[:, 0:3 * P], decay[:, :], ALU.mult)\
                    .then_inc(weighted_ready, 1)

            def head_divide(hd_):
                at = hd_ % 2 * VD
                dve.wait_ge(num_ready, hd_ + 1)
                link(nc.vector.tensor_tensor(den[:, :], den_ps, floor_t[:, :, hd_], ALU.max))
                link(nc.vector.scalar_tensor_tensor(out=den[:, :], in0=den_ps, scalar=-1.0,
                                                    in1=den[:, :], op0=ALU.mult, op1=ALU.max))
                link(nc.vector.reciprocal(den_inv[:, :], den[:, :]))
                for t in range(TT):
                    last = nc.vector.tensor_scalar(heads_out[:, t, at:at + VD],
                                                   num_ps[:, t * VD:(t + 1) * VD],
                                                   den_inv[:, t:t + 1], None, ALU.mult)
                link(last)
                for t in range(TT):
                    link(nc.vector.scalar_tensor_tensor(
                        out=scratch_v[:, :], in0=heads_out[:, t, at:at + VD], scalar=1.0,
                        in1=heads_out[:, t, at:at + VD], op0=ALU.mult, op1=ALU.mult,
                        accum_out=head_sq[:, t:t + 1]))
                nc.vector.tensor_scalar(head_sq[:, :], head_sq[:, :], 1.0 / VD, EPS, ALU.mult, ALU.add)\
                    .then_inc(head_divided, 1)

            def head_norm(hd_):
                at = hd_ % 2 * VD
                dve.wait_ge(head_divided, hd_ + 1)
                link(inverse_root(head_rstd[:, :], head_sq[:, :], head_newton[:, :]))
                for t in range(TT):
                    last = nc.vector.tensor_scalar(heads_out[:, t, at:at + VD], heads_out[:, t, at:at + VD],
                                                   head_rstd[:, t:t + 1], None, ALU.mult)
                last.then_inc(head_ready, 1)

            def gate_heads(p):
                dve.wait_ge(silu_ready, NF + p + 1)
                dve.wait_ge(head_ready, 2 * p + 2)
                nc.vector.tensor_tensor(tile[:, :, :], tile[:, :, :], heads_out[:, :, :], ALU.mult)\
                    .then_inc(tile_ready, 1)

            def low_y(p, half):
                k = 4 * p + 2 * half
                low(R_Y + p, half, y_hi[:, k:k + 2], y_lo[:, k:k + 2], GAIN_HEAD + k)

            for p in range(NV):
                g = G_MIX + (8 + p) * GD
                split(g, 0, 1)
                if p:
                    head_weights(2 * p - 1)
                split(g, 1, 3)
                if p:
                    head_divide(2 * p - 1)
                    head_norm(2 * p - 1)
                    gate_heads(p - 1)
                split(g, 3, 5)
                head_weights(2 * p)
                if p:
                    low_y(p - 1, 0)
                split(g, 5, 7)
                head_divide(2 * p)
                if p:
                    low_y(p - 1, 1)
                head_norm(2 * p)
                split(g, 7, 8)
            g = G_MIX_OUT
            split(g, 0, 1)
            head_weights(HEADS - 1)
            split(g, 1, 3)
            head_divide(HEADS - 1)
            head_norm(HEADS - 1)
            gate_heads(NV - 1)
            split(g, 3, 5)
            low_y(NV - 1, 0)
            split(g, 5, 7)
            low_y(NV - 1, 1)
            split(g, 7, 8)
            for n in range(1, ND):
                g = G_MIX_OUT + n * GD
                r = R_H2 + n - 1
                split(g, 0, 3)
                add_residual(C_MIX_OUT + n - 1, g, r, n - 1, 1.0, 2)
                split(g, 3, 5)
                low_h(r, n - 1, 0, GAIN_FFN[1])
                split(g, 5, 7)
                low_h(r, n - 1, 1, GAIN_FFN[1])
                split(g, 7, 8)

            first_chunk(G_FFN[1], C_FFN[1], R_H2 + ND - 1, GAIN_FFN[1], 1.0, 2)
            split(G_FFN[1], 8, 10)
            dve.wait_ge(rstd_ready, 3)
            ffn_in(1)
            ffn_out(1)
            c, last_cols = C_FFN_OUT[1] + ND - 1, slice((ND - 1) * COLS, D)
            dve.wait_ge(squared, TT * (4 * ND - 1))
            dve.wait_ge(kept, 3 * ND - 1)
            for t in range(TT):
                dve.wait_ge(last_summed, t + 1)
                nc.vector.scalar_tensor_tensor(out=tile[:, t, :], in0=acc[:, TT * (c % 2) + t, :],
                                               scalar=0.5, in1=h[:, t, last_cols],
                                               op0=ALU.mult, op1=ALU.add).then_inc(last_ready, 1)
                rms(3, t, t + 1)
                dve.wait_ge(rstd_ready, 4 + t)
                dve.wait_ge(kept, 3 * ND + t)
                cols = slice(0, D if t == 0 else D // 2)
                nc.vector.tensor_scalar(h[:, t, cols], h[:, t, cols], rstd[:, 3, t:t + 1], None,
                                        ALU.mult).then_inc(vec_out, 1)


_INS = ["x", "ffn_norm", "ffn_w_in", "ffn_w_out", "mix_norm", "a_w_in", "a_b_if", "a_head_norm",
        "a_w_out", "final_norm"]


def kernel(**inputs):
    import numpy as _np
    import concourse.bacc as _bacc
    from concourse import mybir as _mybir
    from concourse.bass_utils import run_bass_kernel_spmd as _run

    nc = _bacc.Bacc("TRN2", target_bir_lowering=False, num_devices=1)
    arrays, args = {}, []
    for name in _INS:
        a = _np.ascontiguousarray(inputs[name])
        arrays[f"in_{name}_dram"] = a
        args.append(nc.dram_tensor(f"in_{name}_dram", a.shape, _mybir.dt.from_np(a.dtype),
                                   kind="ExternalInput").ap())
    shape = inputs["x"].shape
    args.append(nc.dram_tensor("out_0_dram", shape, _mybir.dt.float32, kind="ExternalOutput").ap())
    trunk_program(nc, *args)
    r = _run(nc, [arrays], core_ids=[0])
    return r.results[0]["out_0_dram"]
```
